# Optimizing a Trainium2 kernel written in Bass

```python
import math
import jax, jax.numpy as jnp
from jax import lax
import numpy as np

D_MODEL = 1024
BATCH = 1
SEQ = 256
DEPTH = 2
DEC_BATCH = 8
DEC_SEQ = 8
PAST_LEN = 2048
PAGE_SIZE = 128

N_RET_HEADS = 4
RET_DK = D_MODEL // N_RET_HEADS
RET_DV = 2 * RET_DK
RET_QK = N_RET_HEADS * RET_DK
RET_V = N_RET_HEADS * RET_DV
RET_CHUNK = 128
ROPE_BASE = 10000.0
D_CONV = D_MODEL
CONV_WIDTH = 31
D_FF = ((8 * D_MODEL // 3 + 255) // 256) * 256
N_IN = 2 * RET_QK + 2 * RET_V + 2 * D_CONV + 2 * D_MODEL
EPS = 1e-6

kernel_name = "retnet_conformer_gated_hybrid_step"

def rms_norm(x, g):
    xf = x.astype(jnp.float32)
    y = xf * lax.rsqrt(jnp.mean(xf * xf, axis=-1, keepdims=True) + EPS)
    return (y * g.astype(jnp.float32)).astype(x.dtype)

def layer_norm(x, g, b=None):
    xf = x.astype(jnp.float32)
    mu = jnp.mean(xf, axis=-1, keepdims=True)
    xc = xf - mu
    y = xc * lax.rsqrt(jnp.mean(xc * xc, axis=-1, keepdims=True) + EPS) * g.astype(jnp.float32)
    if b is not None:
        y = y + b.astype(jnp.float32)
    return y.astype(x.dtype)

def rope(x, pos):
    half = x.shape[-1] // 2
    freqs = ROPE_BASE ** (-jnp.arange(half, dtype=jnp.float32) / half)
    ang = pos.astype(jnp.float32)[:, None] * freqs[None, :]
    cos = jnp.cos(ang)[None, :, None, :]
    sin = jnp.sin(ang)[None, :, None, :]
    xf = x.astype(jnp.float32)
    x1, x2 = xf[..., :half], xf[..., half:]
    return jnp.concatenate([x1 * cos - x2 * sin, x1 * sin + x2 * cos], axis=-1)

def ret_log_decay():
    return jnp.log1p(-jnp.exp2(-5.0 - jnp.arange(N_RET_HEADS, dtype=jnp.float32)))

def retention_chunkwise(q, k, v, r0):
    B, T, H, DK = q.shape
    DV = v.shape[-1]
    C = math.gcd(T, RET_CHUNK)
    N = T // C
    log_g = ret_log_decay()
    idx = jnp.arange(C, dtype=jnp.float32)
    diff = idx[:, None] - idx[None, :]
    dmat = jnp.where(diff >= 0, jnp.exp(log_g[:, None, None] * jnp.maximum(diff, 0.0)), 0.0)
    q_decay = jnp.exp(log_g[None, :] * (idx[:, None] + 1.0))
    k_decay = jnp.exp(log_g[None, :] * (C - 1.0 - idx[:, None]))
    chunk_decay = jnp.exp(log_g * C)

    def to_chunks(t):
        return t.reshape(B, N, C, H, t.shape[-1]).transpose(1, 0, 2, 3, 4)

    def step(r, inp):
        qc, kc, vc = inp
        s = jnp.einsum('bihd,bjhd->bhij', qc, kc) * dmat[None]
        inner = jnp.einsum('bhij,bjhe->bihe', s, vc)
        cross = jnp.einsum('bihd,bhde->bihe', qc, r) * q_decay[None, :, :, None]
        r_new = r * chunk_decay[None, :, None, None] + jnp.einsum(
            'bjhd,bjhe->bhde', kc * k_decay[None, :, :, None], vc)
        return r_new, inner + cross

    r_fin, o = lax.scan(step, r0.astype(jnp.float32), (to_chunks(q), to_chunks(k), to_chunks(v)))
    o = o.transpose(1, 0, 2, 3, 4).reshape(B, T, H, DV)
    return o, r_fin

def trunk_layer(x, r0, c0, pos, g_mix_pre, g_mix_post, g_ffn_pre, g_ffn_post, w_in, b_gate,
                ret_gn_gain, w_ret_out, conv_w, conv_b, conv_ln_g, conv_ln_b, w_conv_out, w_o,
                w_ffn_gate, w_ffn_up, w_ffn_down):
    B, T, _ = x.shape
    h = rms_norm(x, g_mix_pre)
    proj = h @ w_in
    offs = np.cumsum([RET_QK, RET_QK, RET_V, RET_V, D_CONV, D_CONV, D_MODEL]).tolist()
    q, k, v, g_ret, ca, cb, ga, gb = jnp.split(proj, offs, axis=-1)

    q = rope(q.reshape(B, T, N_RET_HEADS, RET_DK), pos)
    k = rope(k.reshape(B, T, N_RET_HEADS, RET_DK), pos) * (RET_DK ** -0.5)
    v = v.reshape(B, T, N_RET_HEADS, RET_DV).astype(jnp.float32)
    o, r_new = retention_chunkwise(q, k, v, r0)
    o = layer_norm(o, ret_gn_gain.reshape(N_RET_HEADS, RET_DV))
    o = o.reshape(B, T, RET_V).astype(x.dtype)
    y_ret = (jax.nn.silu(g_ret) * o) @ w_ret_out

    u = ca * jax.nn.sigmoid(cb)
    padded = jnp.concatenate([c0.astype(u.dtype), u], axis=1)
    c_new = padded[:, -(CONV_WIDTH - 1):, :]
    z = lax.conv_general_dilated(
        padded, conv_w[:, None, :].astype(u.dtype), window_strides=(1,), padding='VALID',
        dimension_numbers=('NWC', 'WIO', 'NWC'), feature_group_count=D_CONV) + conv_b
    z = jax.nn.silu(layer_norm(z, conv_ln_g, conv_ln_b))
    y_conv = z @ w_conv_out

    b_ga, b_gb = b_gate[:D_MODEL], b_gate[D_MODEL:]
    merged = jax.nn.sigmoid(ga + b_ga) * y_ret + jax.nn.sigmoid(gb + b_gb) * y_conv
    x = x + rms_norm(merged @ w_o, g_mix_post)

    h2 = rms_norm(x, g_ffn_pre)
    f = (jax.nn.silu(h2 @ w_ffn_gate) * (h2 @ w_ffn_up)) @ w_ffn_down
    x = x + rms_norm(f, g_ffn_post)
    return x, r_new, c_new

def setup_inputs(seed: int = 0) -> dict:
    key = jax.random.key(seed)
    ks = jax.random.split(key, 24)
    f32 = jnp.float32

    def nrm(k, shape, scale):
        return jax.random.normal(k, shape, f32) * scale

    def gain(k, shape):
        return 1.0 + 0.02 * jax.random.normal(k, shape, f32)

    return {
        "x_prompt": nrm(ks[0], (BATCH, SEQ, D_MODEL), 1.0),
        "x_sample": nrm(ks[1], (DEC_BATCH, DEC_SEQ, D_MODEL), 1.0),
        "state_ret": nrm(ks[2], (DEPTH, DEC_BATCH, N_RET_HEADS, RET_DK, RET_DV), 0.5),
        "state_conv": nrm(ks[3], (DEPTH, DEC_BATCH, CONV_WIDTH - 1, D_CONV), 0.5),
        "g_mix_pre": gain(ks[4], (DEPTH, D_MODEL)),
        "g_mix_post": gain(ks[5], (DEPTH, D_MODEL)),
        "g_ffn_pre": gain(ks[6], (DEPTH, D_MODEL)),
        "g_ffn_post": gain(ks[7], (DEPTH, D_MODEL)),
        "w_in": nrm(ks[8], (DEPTH, D_MODEL, N_IN), D_MODEL ** -0.5),
        "b_gate": nrm(ks[9], (DEPTH, 2 * D_MODEL), 0.02),
        "ret_gn_gain": gain(ks[10], (DEPTH, RET_V)),
        "w_ret_out": nrm(ks[11], (DEPTH, RET_V, D_MODEL), RET_V ** -0.5),
        "conv_w": nrm(ks[12], (DEPTH, CONV_WIDTH, D_CONV), CONV_WIDTH ** -0.5),
        "conv_b": nrm(ks[13], (DEPTH, D_CONV), 0.02),
        "conv_ln_g": gain(ks[14], (DEPTH, D_CONV)),
        "conv_ln_b": nrm(ks[15], (DEPTH, D_CONV), 0.02),
        "w_conv_out": nrm(ks[16], (DEPTH, D_CONV, D_MODEL), D_CONV ** -0.5),
        "w_o": nrm(ks[17], (DEPTH, D_MODEL, D_MODEL), D_MODEL ** -0.5),
        "w_ffn_gate": nrm(ks[18], (DEPTH, D_MODEL, D_FF), D_MODEL ** -0.5),
        "w_ffn_up": nrm(ks[19], (DEPTH, D_MODEL, D_FF), D_MODEL ** -0.5),
        "w_ffn_down": nrm(ks[20], (DEPTH, D_FF, D_MODEL), D_FF ** -0.5),
    }

def reference(x_prompt, x_sample, state_ret, state_conv, g_mix_pre, g_mix_post, g_ffn_pre,
              g_ffn_post, w_in, b_gate, ret_gn_gain, w_ret_out, conv_w, conv_b, conv_ln_g,
              conv_ln_b, w_conv_out, w_o, w_ffn_gate, w_ffn_up, w_ffn_down):
    pos_prompt = jnp.arange(SEQ, dtype=jnp.int32)
    pos_sample = PAST_LEN + jnp.arange(DEC_SEQ, dtype=jnp.int32)
    xp, xs = x_prompt, x_sample
    rp_list, cp_list, rs_list, cs_list = [], [], [], []
    for l in range(DEPTH):
        params = (g_mix_pre[l], g_mix_post[l], g_ffn_pre[l], g_ffn_post[l], w_in[l], b_gate[l],
                  ret_gn_gain[l], w_ret_out[l], conv_w[l], conv_b[l], conv_ln_g[l], conv_ln_b[l],
                  w_conv_out[l], w_o[l], w_ffn_gate[l], w_ffn_up[l], w_ffn_down[l])
        r0_p = jnp.zeros((BATCH, N_RET_HEADS, RET_DK, RET_DV), jnp.float32)
        c0_p = jnp.zeros((BATCH, CONV_WIDTH - 1, D_CONV), x_prompt.dtype)
        xp, rp, cp = trunk_layer(xp, r0_p, c0_p, pos_prompt, *params)
        xs, rs, cs = trunk_layer(xs, state_ret[l], state_conv[l], pos_sample, *params)
        rp_list.append(rp.astype(x_prompt.dtype))
        cp_list.append(cp.astype(x_prompt.dtype))
        rs_list.append(rs.astype(state_ret.dtype))
        cs_list.append(cs.astype(state_conv.dtype))
    new_state_ret_prompt = jnp.stack(rp_list, axis=0)
    new_state_conv_prompt = jnp.stack(cp_list, axis=0)
    new_state_ret_sample = jnp.stack(rs_list, axis=0)
    new_state_conv_sample = jnp.stack(cs_list, axis=0)
    return (xp, xs, new_state_ret_prompt, new_state_conv_prompt, new_state_ret_sample, new_state_conv_sample)


_drawn_inputs = setup_inputs


def setup_inputs(seed=0):
    import zlib

    import numpy as np

    out = dict(_drawn_inputs(seed))
    spreads = {}
    factors = {'g_ffn_post': 3.184,
     'b_gate': 5.913,
     'ret_gn_gain': 3.303,
     'conv_ln_g': 2.692,
     'conv_ln_b': 3.048}
    for name, (base, spread) in spreads.items():
        noise = np.random.default_rng([zlib.crc32(name.encode()), seed]).standard_normal(out[name].shape)
        drawn = base * np.exp(spread * noise) if base else spread * noise
        out[name] = __import__('jax').numpy.asarray(drawn.astype(out[name].dtype))
    for name, factor in factors.items():
        out[name] = (out[name] * factor).astype(out[name].dtype)
    return out
```

```python
import math
from contextlib import ExitStack

import numpy as np

import concourse.bass as bass
from concourse import mybir

F32 = mybir.dt.float32
ALU = mybir.AluOpType
ACT = mybir.ActivationFunctionType
ds = bass.ds

P = 128
D = 1024
DEPTH = 2
SEQ = 256
DB, DS = 8, 8
PAST = 2048
T = SEQ + DB * DS
HEADS = 4
DK, DV = 256, 512
TAPS = 31
PAD = TAPS - 1
FF = 2816
EPS = 1e-6
KT = D // P
FT = FF // P
VT = HEADS * DV // P
UB = 8
RING = 4

U_CIN, U_HEAD, U_GB, U_RET, U_CO, U_WO, U_GU, U_DOWN, UNITS = 0, 16, 64, 72, 96, 104, 112, 156, 180
HEAD_UNITS = 12
SIGS, SIG_G, SIG_GB, SIG_GA, SIG_GATE = 62, 8, 24, 32, 40
SQS, SQ_RET, SQ_CONV, SQ_POST, SQ_FFN, SQ_POST2 = 44, 8, 12, 20, 28, 36
STATS, ST_X, ST_CMEAN, ST_CVAR, ST_POST, ST_FFN, ST_POST2 = 10, 1, 5, 6, 7, 8, 9
RSTDS, RS_RET, RS_CONV, RS_POST, RS_FFN, RS_POST2 = 9, 1, 5, 6, 7, 8
AUX_HEAD, AUX_ACT, AUX_DVE = 28, 8, 20
ROPES, CONVS = 12, 2 * TAPS

A_KT, A_KTS, A_V, A_S, A_P, A_U, A_PU, A_MEAN, A_VAR = 0, 1, 2, 5, 6, 8, 24, 26, 27
READER = ([("dve", 0), ("dve", 1), ("act", 0), ("act", 1), ("act", 2), ("dve", 2), ("act", 3), ("act", 4)]
          + [("dve", 3 + i) for i in range(16)] + [("act", 5), ("act", 6), ("dve", 19), ("act", 7)])
BEFORE = {0: 27, 1: 25, 2: 26}

C_COS, C_SIN, C_MASK, C_KDEC, C_KMASK, C_QDEC, C_CD, C_ID = 0, 320, 640, 2432, 2440, 2472, 2728, 2732
NCONST = C_ID + P
MASKW = 448
G_MIXPRE, G_MIXPOST, G_FFNPRE, G_FFNPOST, G_GATE, G_RET, G_CB, G_LNG, G_LNB, G_CW = 0, 8, 16, 24, 32, 48, 64, 72, 80, 88
NPAR = G_CW + KT * TAPS


def program(nc, w, xin, consts, params, r_in, c_in, x_out, rp_out, rs_out, cp_out, cs_out):
    ctx = ExitStack()
    with ctx:
        def sb(name, *shape):
            return ctx.enter_context(nc.sbuf_tensor(name, [P, *shape], F32))

        def sem(name):
            return ctx.enter_context(nc.semaphore(name))

        wring = [sb(f"wring{i}", UB, P) for i in range(RING)]
        x = sb("x", KT, T)
        h = sb("h", KT, T)
        acc = sb("acc", KT, T)
        acc2 = sb("acc2", KT, T)
        wide = sb("wide", KT + VT, T)
        zt, go, f = wide[:, 0:KT, :], wide[:, KT:KT + VT, :], wide[:, 0:FT, :]
        qkv = sb("qkv", 8, T)
        sg = sb("sg", 4, T)
        sgb = sb("sgb", KT, T)
        up = sb("up", KT, SEQ + PAD)
        us = sb("us", KT, DB, DS + PAD)
        kdec = sb("kdec", 2, DK)
        kdecs = sb("kdecs", DB, DK)
        vtok = sb("vtok", 3, DV)
        stm = sb("stm", MASKW)
        qd = sb("qd", 2, DB * DS)
        oT = sb("oT", 4, T)
        sqo = sb("sqo", 4, T)
        rstd = sb("rstd", T)
        lnv = sb("lnv", T)
        cmean = sb("cmean", T)
        sig = sb("sig", 4, T)
        tmp = sb("tmp", 4, T)
        state = [sb(f"state{i}", 2, DV) for i in range(RING)]
        pst = sb("pst", 2, DV)
        con = sb("con", NCONST)
        par_all = sb("par_all", DEPTH, NPAR)
        par = sb("par", NPAR)
        ones_d = sb("ones_d", P)
        ones_v = sb("ones_v", P)
        eps = sb("eps", 1)

        bank = [ctx.enter_context(nc.psum_tensor(f"bank{i}", [P, 512], F32)) for i in range(8)]
        aux = bank[4:7]
        X = bank[7]

        w_ready = [sem(f"w_ready{i}") for i in range(RING)]
        unit_done = sem("unit_done")
        aux_done = sem("aux_done")
        stat_done = sem("stat_done")
        sig_done = sem("sig_done")
        v_copied = sem("v_copied")
        sq_done = sem("sq_done")
        stat_read = sem("stat_read")
        rstd_done = sem("rstd_done")
        act_aux = sem("act_aux")
        zsig_done = sem("zsig_done")
        dve_aux = sem("dve_aux")
        par_ready = sem("par_ready")
        memset_done = sem("memset_done")
        h_ready = sem("h_ready")
        u_ready = sem("u_ready")
        rope_step = sem("rope_step")
        qd_ready = sem("qd_ready")
        sg_ready = sem("sg_ready")
        ret_norm = sem("ret_norm")
        conv_step = sem("conv_step")
        conv_norm = sem("conv_norm")
        ret_gated = sem("ret_gated")
        merge_step = sem("merge_step")
        y_copied = sem("y_copied")
        post_step = sem("post_step")
        ffn_step = sem("ffn_step")
        in_loaded = sem("in_loaded")
        u_loaded = sem("u_loaded")
        u_saved = sem("u_saved")
        r_loaded = [sem(f"r_loaded{i}") for i in range(RING)]
        r_stored = [sem(f"r_stored{i}") for i in range(RING)]
        pst_stored = sem("pst_stored")
        x_stored = sem("x_stored")

        def col(c0, n):
            return con[:, c0:c0 + n]

        def g_(c):
            return par[:, c:c + 1]

        block = ctx.enter_context(nc.Block())

        @block.sync
        def _(sp):
            for s in range(RING):
                sp.dma_start(wring[s][:, :, :], w[s]).then_inc(w_ready[s], 16)
            with sp.Fori(1, DEPTH * UNITS // RING) as i:
                for s in range(RING):
                    sp.wait_ge(unit_done, i * RING + (s + 1 - RING))
                    sp.dma_start(wring[s][:, :, :], w[i * RING + s]).then_inc(w_ready[s], 16)

        @block.gpsimd
        def _(pool):
            pool.dma_start(x[:, :, :], xin).then_inc(in_loaded, 16)
            pool.dma_start(par_all[:, :, :], params).then_inc(in_loaded, 16)
            pool.dma_start(con[:, :], consts).then_inc(in_loaded, 16)

            def load(l, j, s):
                pool.dma_start(state[s][:, :, :], r_in[l * (HEADS * DB) + j]).then_inc(r_loaded[s], 16)

            def head(l, hd, last):
                for b in range(DB):
                    pool.wait_ge(dve_aux, (l * HEADS + hd) * AUX_DVE + (3 + 2 * b + 2))
                    s = b % RING
                    pool.dma_start(rs_out[(l * HEADS + hd) * DB + b], state[s][:, :, :]).then_inc(r_stored[s], 16)
                    if b and not (last and b > RING):
                        pool.wait_ge(r_stored[(b - 1) % RING], (l * HEADS + hd) * 32 + 16 * ((b - 1) // RING + 1))
                        load(l, hd * DB + (b - 1 + RING), (b - 1) % RING)
                if not last:
                    pool.wait_ge(r_stored[RING - 1], (l * HEADS + hd) * 32 + 32)
                    load(l, hd * DB + (DB - 1 + RING), RING - 1)
                pool.wait_ge(act_aux, (l * HEADS + hd) * AUX_ACT + 7)
                pool.dma_start(rp_out[l * HEADS + hd], pst[:, :, :]).then_inc(pst_stored, 16)

            with pool.Fori(0, DEPTH) as l:
                pool.dma_start(us[:, :, :, :], c_in[l]).then_inc(u_loaded, 16)
                for s in range(RING):
                    load(l, s, s)
                pool.wait_ge(u_ready, l * 16 + 16)
                pool.dma_start(cp_out[l], up[:, :, :]).then_inc(u_saved, 16)
                pool.dma_start(cs_out[l], us[:, :, :, :]).then_inc(u_saved, 16)
                with pool.Fori(0, HEADS - 1) as hd:
                    head(l, hd, False)
                head(l, HEADS - 1, True)
                pool.wait_ge(u_saved, l * 32 + 32)
                pool.wait_ge(conv_step, l * (KT * CONVS) + KT * CONVS)
                for s in range(RING):
                    pool.wait_ge(r_stored[s], l * (HEADS * 32) + HEADS * 32)
            pool.wait_ge(post_step, DEPTH * 32)
            pool.dma_start(x_out, x[:, :, :]).then_inc(x_stored, 16)
            pool.wait_ge(x_stored, 16)
            pool.wait_ge(pst_stored, DEPTH * HEADS * 16)

        @block.tensor
        def _(pe):
            def unit(l, q, j, g, rhs, k0=0, n=UB, start=True, stop=True, ready=None):
                pe.wait_ge(w_ready[j], (l * (UNITS // RING) + q + 1) * 16)
                for k in range(n):
                    if ready is not None:
                        ready(k0 + k)
                    mm = pe.matmul(bank[g][:, 0:T], wring[j][:, k, :], rhs(k0 + k),
                                   start=start and k == 0, stop=stop and k == n - 1)
                mm.then_inc(unit_done, 1)

            def h_tile(k):
                return h[:, k, :]

            def stat(l, i, src, n, ones, sq=None, out=X):
                for k in range(n):
                    if sq is not None:
                        sq(k)
                    mm = pe.matmul(out[:, 0:T], ones[:, :], src(k), start=(k == 0), stop=(k == n - 1))
                return mm

            def aux_free(H, pos, first=False):
                if pos >= 3:
                    who, n = READER[pos - 3]
                elif first:
                    return
                else:
                    who, n = READER[BEFORE[pos]]
                    H = H - 1
                if who == "act":
                    pe.wait_ge(act_aux, H * AUX_ACT + (n + 1))
                else:
                    pe.wait_ge(dve_aux, H * AUX_DVE + (n + 1))

            def early(l, hd, first=False):
                H = l * HEADS + hd
                ident = con[:, C_ID:C_ID + P]
                aux_free(H, A_KT, first)
                aux_free(H, A_KTS, first)
                pe.wait_ge(rope_step, H * ROPES + ROPES)
                for c in range(2):
                    for d in range(2):
                        mm = pe.transpose(aux[0][:, c * DK + d * P:c * DK + (d + 1) * P], qkv[:, 2 + d, c * P:(c + 1) * P], ident)
                mm.then_inc(aux_done, 1)
                for d in range(2):
                    mm = pe.transpose(aux[1][0:64, d * P:(d + 1) * P], qkv[:, 2 + d, SEQ:T], ident)
                mm.then_inc(aux_done, 1)
                pe.wait_ge(v_copied, H * 4 + 4)
                for c in range(3):
                    n = P if c < 2 else T - SEQ
                    if c < 2:
                        aux_free(H, A_V + c, first)
                    if c == 1:
                        aux_free(H, A_V + 2)
                    for e in range(4):
                        mm = pe.transpose(aux[(A_V + c) % 3][0:n, e * P:(e + 1) * P], qkv[:, 4 + e, c * P:c * P + n], ident)
                    mm.then_inc(aux_done, 1)
                aux_free(H, A_S)
                b = aux[A_S % 3]
                for o, j0, n, i0, m in ((0, 0, P, 0, SEQ), (SEQ, P, P, P, P), (SEQ + P, SEQ, 64, SEQ, 64)):
                    for d in range(2):
                        mm = pe.matmul(b[0:n, o:o + m], qkv[:, 2 + d, j0:j0 + n], qkv[:, d, i0:i0 + m],
                                       start=(d == 0), stop=(d == 1))
                mm.then_inc(aux_done, 1)

            def late_out(l, hd):
                H = l * HEADS + hd
                pe.wait_ge(dve_aux, H * AUX_DVE + 3)
                pe.wait_ge(act_aux, H * AUX_ACT + 3)
                for p in range(2):
                    aux_free(H, A_P + p)
                    for i in range(2):
                        e = 2 * p + i
                        o = aux[(A_P + p) % 3]
                        pe.matmul(o[:, i * SEQ:(i + 1) * SEQ], vtok[:, 0, e * P:(e + 1) * P], stm[:, 0:SEQ], start=True, stop=False)
                        mm = pe.matmul(o[:, i * SEQ + P:(i + 1) * SEQ], vtok[:, 1, e * P:(e + 1) * P], stm[:, SEQ:SEQ + P],
                                       start=False, stop=True)
                    mm.then_inc(aux_done, 1)
                pe.wait_ge(qd_ready, H + 1)
                for e in range(4):
                    pe.matmul(X[:, e * 64:(e + 1) * 64], vtok[0:64, 2, e * P:(e + 1) * P], stm[0:64, SEQ + P:MASKW],
                              start=(e == 0), stop=False, skip_group_check=True)

            def late_state(l, hd, b):
                H = l * HEADS + hd
                s = b % RING
                pe.wait_ge(r_loaded[s], H * 32 + (b // RING + 1) * 16)
                for e in range(4):
                    for d in range(2):
                        mm = pe.matmul(X[:, e * 64 + b * DS:e * 64 + (b + 1) * DS], state[s][:, d, e * P:(e + 1) * P],
                                       qd[:, d, b * DS:(b + 1) * DS], start=False, stop=(d == 1), skip_group_check=True)
                if b == DB - 1:
                    mm.then_inc(stat_done, 1)
                for d in range(2):
                    pos = A_U + 2 * b + d
                    aux_free(H, pos)
                    pe.matmul(aux[pos % 3][:, :], kdecs[0:64, b, d * P:(d + 1) * P], vtok[0:64, 2, :],
                              start=True, stop=True).then_inc(aux_done, 1)

            def late_prompt_state(l, hd):
                H = l * HEADS + hd
                for d in range(2):
                    pos = A_PU + d
                    aux_free(H, pos)
                    for c in range(2):
                        mm = pe.matmul(aux[pos % 3][:, :], kdec[:, c, d * P:(d + 1) * P], vtok[:, c, :],
                                       start=(c == 0), stop=(c == 1))
                    mm.then_inc(aux_done, 1)

            def late_mean(l, hd):
                H = l * HEADS + hd
                aux_free(H, A_MEAN)
                pe.wait_ge(act_aux, H * AUX_ACT + 5)
                pe.wait_ge(stat_read, l * STATS + (hd + (ST_X + 1)))
                stat(l, 0, lambda k: oT[:, k, :], 4, ones_v, out=aux[A_MEAN % 3]).then_inc(aux_done, 1)

            def late_var(l, hd):
                H = l * HEADS + hd
                aux_free(H, A_VAR)
                pe.wait_ge(sq_done, l * SQS + (hd + (SQ_RET + 1)))
                stat(l, 0, lambda k: sqo[:, k, :], 4, ones_v, out=aux[A_VAR % 3]).then_inc(aux_done, 1)

            def late(l, hd, j):
                if j == 0:
                    late_out(l, hd)
                if j < 4:
                    late_state(l, hd, 2 * j)
                    late_state(l, hd, 2 * j + 1)
                if j == 4:
                    late_prompt_state(l, hd)
                if j == 5:
                    late_mean(l, hd)
                if j == 7:
                    late_var(l, hd)

            def head(l, hd, first):
                H = l * HEADS + hd
                for j in range(HEAD_UNITS):
                    if j < 4 and first:
                        if j % 2 == 0:
                            pe.wait_ge(sig_done, l * SIGS + (7 + j // 2))
                        else:
                            pe.wait_ge(u_ready, l * 16 + (14 + j - 1))
                    elif j < 4:
                        pe.wait_ge(sg_ready, H * 4 + (j + 1 - 4))
                    elif j < 8:
                        pe.wait_ge(rope_step, H * ROPES + (3, 4, 9, 10)[j - 4])
                    else:
                        pe.wait_ge(v_copied, H * 4 + (j - 7))
                    unit(l, hd * 3 + (U_HEAD // RING + j // RING), j % RING, j % 4, h_tile)
                    if not first:
                        late(l, hd - 1, j)
                early(l, hd, first)

            def h_read(l, k):
                pe.wait_ge(h_ready, l * 16 + (k + 1))

            pe.wait_ge(in_loaded, 48)
            pe.wait_ge(memset_done, 4)
            with pe.Fori(0, DEPTH) as l:
                stat(l, 0, lambda k: qkv[:, k, :], KT, ones_d, lambda k: pe.wait_ge(sq_done, l * SQS + (k + 1))).then_inc(stat_done, 1)
                for j in range(4):
                    unit(l, 0, j, j, h_tile, ready=(lambda k: h_read(l, k)) if j == 0 else None)
                with pe.Fori(1, 4) as i:
                    for j in range(4):
                        if j % 2 == 0:
                            pe.wait_ge(sig_done, l * SIGS + i * 2 + (j // 2 - 1))
                        else:
                            pe.wait_ge(u_ready, l * 16 + i * 4 + (j - 3))
                        unit(l, i, j, j, h_tile)
                head(l, 0, True)
                with pe.Fori(1, HEADS) as hd:
                    head(l, hd, False)
                for n in range(KT):
                    if n < 4:
                        pe.wait_ge(sg_ready, l * 16 + (13 + n))
                    else:
                        pe.wait_ge(sig_done, l * SIGS + (SIG_GB + n - 3))
                    u = U_GB + n
                    unit(l, u // RING, u % RING, n % 4, h_tile)
                    late(l, HEADS - 1, n)
                for n in range(KT):
                    g = (2 * n) % 4
                    if n < 2:
                        pe.wait_ge(sig_done, l * SIGS + (SIG_GB + 5 + 2 * n))
                    else:
                        pe.wait_ge(sig_done, l * SIGS + (SIG_GA + n - 1))
                    u = U_RET + 3 * n
                    unit(l, u // RING, u % RING, g, h_tile)
                    if n < 2:
                        pe.wait_ge(sig_done, l * SIGS + (SIG_GB + 6 + 2 * n))
                    else:
                        pe.wait_ge(ret_gated, l * 8 + (n - 1))
                    if n == 0:
                        pe.wait_ge(ret_norm, l * (HEADS * 6) + HEADS * 6)
                    for p in range(2):
                        u = U_RET + 3 * n + 1 + p
                        unit(l, u // RING, u % RING, g + 1, lambda k: go[:, k, :], k0=8 * p, start=(p == 0), stop=(p == 1))
                    if n == 1:
                        pe.wait_ge(conv_step, l * (KT * CONVS) + KT * CONVS)
                        stat(l, 0, lambda k: acc[:, k, :], KT, ones_d).then_inc(stat_done, 1)
                    if n == 4:
                        pe.wait_ge(stat_read, l * STATS + (ST_CMEAN + 1))
                        stat(l, 0, lambda k: qkv[:, k, :], KT, ones_d,
                             lambda k: pe.wait_ge(sq_done, l * SQS + (SQ_CONV + k + 1))).then_inc(stat_done, 1)
                for n in range(KT):
                    if n < 4:
                        if n % 2 == 0:
                            pe.wait_ge(sig_done, l * SIGS + (SIG_GA + 7 + n // 2))
                        else:
                            pe.wait_ge(ret_gated, l * 8 + (7 + n // 2))
                    else:
                        pe.wait_ge(merge_step, l * 16 + (2 * (n - 4) + 1))
                    u = U_CO + n
                    unit(l, u // RING, u % RING, n % 4, lambda k: zt[:, k, :],
                         ready=(lambda k: pe.wait_ge(conv_norm, l * 24 + (16 + k + 1))) if n == 0 else None)
                for n in range(KT):
                    if n < 4:
                        pe.wait_ge(merge_step, l * 16 + (2 * (n + 4) + 1))
                    else:
                        pe.wait_ge(y_copied, l * 16 + (n - 3))
                    u = U_WO + n
                    unit(l, u // RING, u % RING, n % 4, h_tile,
                         ready=(lambda k: pe.wait_ge(merge_step, l * 16 + (2 * k + 2))) if n == 0 else None)
                pe.wait_ge(stat_read, l * STATS + (ST_CVAR + 1))
                stat(l, 0, lambda k: qkv[:, k, :], KT, ones_d,
                     lambda k: pe.wait_ge(sq_done, l * SQS + (SQ_POST + k + 1))).then_inc(stat_done, 1)
                pe.wait_ge(stat_read, l * STATS + (ST_POST + 1))
                stat(l, 0, lambda k: qkv[:, k, :], KT, ones_d,
                     lambda k: pe.wait_ge(sq_done, l * SQS + (SQ_FFN + k + 1))).then_inc(stat_done, 1)
                for j in range(4):
                    unit(l, U_GU // RING, j, j, h_tile, ready=(lambda k: h_read(l, 8 + k)) if j == 0 else None)
                with pe.Fori(1, FT // 2) as i:
                    for j in range(4):
                        pe.wait_ge(ffn_step, l * (2 * FT) + i * 4 + (j - 3))
                        unit(l, i + U_GU // RING, j, j, h_tile)
                for n in range(KT):
                    if n < 4:
                        pe.wait_ge(ffn_step, l * (2 * FT) + (2 * FT - 3 + n))
                    else:
                        pe.wait_ge(y_copied, l * 16 + (8 + n - 3))
                    for p in range(3):
                        u = U_DOWN + 3 * n + p
                        unit(l, u // RING, u % RING, n % 4, lambda k: f[:, k, :], k0=8 * p, n=min(8, FT - 8 * p),
                             start=(p == 0), stop=(p == 2),
                             ready=(lambda k: pe.wait_ge(ffn_step, l * (2 * FT) + (2 * k + 2))) if n == 0 else None)
                pe.wait_ge(stat_read, l * STATS + (ST_FFN + 1))
                stat(l, 0, lambda k: qkv[:, k, :], KT, ones_d,
                     lambda k: pe.wait_ge(sq_done, l * SQS + (SQ_POST2 + k + 1))).then_inc(stat_done, 1)

        @block.scalar
        def _(act):
            def gemm(l, u):
                act.wait_ge(unit_done, l * UNITS + (u + 1))

            def rsqrt(l, src, st, rs, aux_read=None):
                if not (isinstance(rs, int) and rs == 0):
                    act.wait_ge(rstd_done, l * RSTDS + rs)
                ln = act.activation(lnv[:, :], src, ACT.Ln, bias=eps[:, 0:1])
                if aux_read is None:
                    ln.then_inc(stat_read, 1)
                    act.wait_ge(stat_read, l * STATS + (st + 1))
                else:
                    ln.then_inc(act_aux, 1)
                    act.wait_ge(act_aux, aux_read)
                act.activation(rstd[:, :], lnv[:, :], ACT.Exp, scale=-0.5).then_inc(rstd_done, 1)

            def sigmoid(dst, src, bias=None):
                if bias is None:
                    act.activation(dst, src, ACT.Sigmoid).then_inc(sig_done, 1)
                else:
                    act.activation(dst, src, ACT.Sigmoid, bias=bias).then_inc(sig_done, 1)

            def late(l, hd, j):
                H = l * HEADS + hd
                if j == 0:
                    for p in range(2):
                        act.wait_ge(aux_done, H * AUX_HEAD + (A_P + p + 1))
                        act.activation(oT[:, 2 * p:2 * p + 2, 0:SEQ], aux[(A_P + p) % 3][:, :].rearrange("p (e t) -> p e t", e=2),
                                       ACT.Copy).then_inc(act_aux, 1)
                if j == 3:
                    act.wait_ge(stat_done, l * STATS + (hd + (ST_X + 1)))
                    act.activation(oT[:, :, SEQ:T], X[:, 0:256].rearrange("p (e t) -> p e t", e=4), ACT.Copy).then_inc(stat_read, 1)
                if j == 4:
                    for d in range(2):
                        act.wait_ge(aux_done, H * AUX_HEAD + (A_PU + d + 1))
                        act.activation(pst[:, d, :], aux[(A_PU + d) % 3][:, :], ACT.Copy).then_inc(act_aux, 1)
                if j == 6:
                    act.wait_ge(dve_aux, H * AUX_DVE + 20)
                    act.activation(sqo[:, :, :], oT[:, :, :], ACT.Square).then_inc(sq_done, 1)
                if j == 8:
                    act.wait_ge(aux_done, H * AUX_HEAD + (A_VAR + 1))
                    rsqrt(l, aux[A_VAR % 3][:, 0:T], None, hd + RS_RET, aux_read=H * AUX_ACT + 8)

            def head(l, hd, first):
                H = l * HEADS + hd
                for j in range(HEAD_UNITS):
                    if not first and j < 8:
                        late(l, hd - 1, j)
                    if 4 <= j < 8:
                        if j == 4 and not first:
                            act.wait_ge(aux_done, H * AUX_HEAD + (A_V + 3 - AUX_HEAD))
                        act.wait_ge(unit_done, l * UNITS + hd * HEAD_UNITS + (U_HEAD + j + 1))
                        act.activation(qkv[:, j, :], bank[j % 4][:, 0:T], ACT.Copy).then_inc(v_copied, 1)
                    if j == 8 and not first:
                        late(l, hd - 1, 8)
                    if j >= 8:
                        if first:
                            act.wait_ge(u_ready, l * 16 + (2 * (j - 4) + 2))
                        else:
                            act.wait_ge(sg_ready, H * 4 + (j - 7 - 4))
                        act.wait_ge(unit_done, l * UNITS + hd * HEAD_UNITS + (U_HEAD + j + 1))
                        sigmoid(sig[:, j - 8, :], bank[j % 4][:, 0:T])
                if not first:
                    act.wait_ge(ret_norm, H * 6)
                    act.wait_ge(pst_stored, H * 16)
                for c in range(3):
                    n = P if c < 2 else T - SEQ
                    act.wait_ge(aux_done, H * AUX_HEAD + (A_V + c + 1))
                    act.activation(vtok[0:n, c, :], aux[(A_V + c) % 3][0:n, :], ACT.Copy).then_inc(act_aux, 1)

            def squares_of_products(l, u0, ustep, sq0, yc0):
                for n in range(KT):
                    act.wait_ge(unit_done, l * UNITS + (u0 + ustep * n + ustep))
                    act.activation(qkv[:, n, :], bank[n % 4][:, 0:T], ACT.Square).then_inc(sq_done, 1)

            act.wait_ge(in_loaded, 48)
            act.wait_ge(memset_done, 4)
            with act.Fori(0, DEPTH) as l:
                for k in range(KT):
                    act.activation(qkv[:, k, :], x[:, k, :], ACT.Square).then_inc(sq_done, 1)
                act.wait_ge(stat_done, l * STATS + 1)
                rsqrt(l, X[:, 0:T], 0, 0)
                act.wait_ge(par_ready, l + 1)
                for n in range(4):
                    gemm(l, U_CIN + 2 * n)
                    sigmoid(sig[:, n, :], bank[(2 * n) % 4][:, 0:T])
                for n in range(4, 8):
                    act.wait_ge(u_ready, l * 16 + (2 * (n - 4) + 2))
                    gemm(l, U_CIN + 2 * n)
                    sigmoid(sig[:, n % 4, :], bank[(2 * n) % 4][:, 0:T])
                head(l, 0, True)
                with act.Fori(1, HEADS) as hd:
                    head(l, hd, False)
                for n in range(KT):
                    gemm(l, U_GB + n)
                    sigmoid(sgb[:, n, :], bank[n % 4][:, 0:T], bias=g_(G_GATE + 8 + n))
                    if n != 7:
                        late(l, HEADS - 1, n)
                late(l, HEADS - 1, 8)
                for n in range(KT):
                    if n < 4:
                        act.wait_ge(sg_ready, l * 16 + (12 + n + 1))
                    else:
                        act.wait_ge(ret_gated, l * 8 + (n - 3))
                    gemm(l, U_RET + 3 * n)
                    sigmoid(sig[:, n % 4, :], bank[(2 * n) % 4][:, 0:T], bias=g_(G_GATE + n))
                    if n == 2:
                        act.wait_ge(stat_done, l * STATS + (ST_CMEAN + 1))
                        act.activation(cmean[:, :], X[:, 0:T], ACT.Copy).then_inc(stat_read, 1)
                    if n == 3:
                        for k in range(KT):
                            act.wait_ge(conv_norm, l * 24 + (k + 1))
                            act.activation(qkv[:, k, :], acc[:, k, :], ACT.Square).then_inc(sq_done, 1)
                    if n == 5:
                        act.wait_ge(stat_done, l * STATS + (ST_CVAR + 1))
                        rsqrt(l, X[:, 0:T], ST_CVAR, RS_CONV)
                for k in range(KT):
                    act.wait_ge(conv_norm, l * 24 + (8 + k + 1))
                    if k < 4:
                        act.wait_ge(ret_gated, l * 8 + (k + 5))
                    else:
                        act.wait_ge(conv_norm, l * 24 + (16 + k - 3))
                    act.activation(sig[:, k % 4, :], zt[:, k, :], ACT.Sigmoid, bias=g_(G_LNB + k)).then_inc(zsig_done, 1)
                squares_of_products(l, U_WO, 1, SQ_POST, 0)
                act.wait_ge(stat_done, l * STATS + (ST_POST + 1))
                rsqrt(l, X[:, 0:T], ST_POST, RS_POST)
                for k in range(KT):
                    act.wait_ge(post_step, l * 32 + (2 * k + 2))
                    act.activation(qkv[:, k, :], x[:, k, :], ACT.Square).then_inc(sq_done, 1)
                act.wait_ge(stat_done, l * STATS + (ST_FFN + 1))
                rsqrt(l, X[:, 0:T], ST_FFN, RS_FFN)
                for n in range(FT):
                    if n >= 4:
                        act.wait_ge(ffn_step, l * (2 * FT) + (2 * (n - 4) + 1))
                    gemm(l, U_GU + 2 * n)
                    sigmoid(sig[:, n % 4, :], bank[(2 * n) % 4][:, 0:T])
                squares_of_products(l, U_DOWN, 3, SQ_POST2, 8)
                act.wait_ge(stat_done, l * STATS + (ST_POST2 + 1))
                rsqrt(l, X[:, 0:T], ST_POST2, RS_POST2)
                act.wait_ge(rstd_done, l * RSTDS + RSTDS)
                act.wait_ge(pst_stored, l * (HEADS * 16) + HEADS * 16)
                act.wait_ge(post_step, l * 32 + 32)

        @block.vector
        def _(dve):
            def us_window(n, k):
                return us[:, n, :, k:k + DS]

            def conv_tap(l, pair, k):
                for i in range(2):
                    n = pair * 2 + i
                    tap = par[:, ds(n * TAPS + (G_CW + k), 1)]
                    a = acc[:, ds(n, 1), :].rearrange("p o t -> p (o t)")
                    pin = up[:, ds(n, 1), k:k + SEQ].rearrange("p o t -> p (o t)")
                    sin = us[:, ds(n, 1), :, k:k + DS].rearrange("p o b t -> p (o b) t")
                    pout, sout = a[:, 0:SEQ], a[:, SEQ:T].rearrange("p (b t) -> p b t", b=DB)
                    if k == 0:
                        bias = par[:, ds(n + G_CB, 1)]
                        dve.tensor_scalar(pout, pin, tap, bias, ALU.mult, ALU.add).then_inc(conv_step, 1)
                        dve.tensor_scalar(sout, sin, tap, bias, ALU.mult, ALU.add).then_inc(conv_step, 1)
                    else:
                        done = l * (KT * CONVS) + pair * (2 * CONVS) + (4 * (k - 1) + 2 * i)
                        dve.wait_ge(conv_step, done + 1)
                        dve.scalar_tensor_tensor(out=pout, in0=pin, scalar=tap, in1=pout, op0=ALU.mult, op1=ALU.add).then_inc(conv_step, 1)
                        dve.wait_ge(conv_step, done + 2)
                        dve.scalar_tensor_tensor(out=sout, in0=sin, scalar=tap, in1=sout, op0=ALU.mult, op1=ALU.add).then_inc(conv_step, 1)

            def conv_taps(l, pair, a, b):
                for k in range(a, b):
                    conv_tap(l, pair, k)

            def rope(l, hd, i, first):
                H = l * HEADS + hd
                base = H * ROPES + 6 * i
                x1, x2 = bank[2 * i][:, 0:T], bank[2 * i + 1][:, 0:T]
                dve.wait_ge(unit_done, l * UNITS + hd * HEAD_UNITS + (U_HEAD + 2 * i + 2))
                if i == 1:
                    dve.wait_ge(rope_step, base)
                cos, sin = col(C_COS, T), col(C_SIN, T)
                for n, (a, b) in enumerate(((x1, cos), (x2, sin), (x1, sin), (x2, cos))):
                    dve.tensor_tensor(tmp[:, n, :], a, b, ALU.mult).then_inc(rope_step, 1)
                dve.wait_ge(rope_step, base + 2)
                dve.tensor_tensor(qkv[:, 2 * i, :], tmp[:, 0, :], tmp[:, 1, :], ALU.subtract).then_inc(rope_step, 1)
                dve.wait_ge(rope_step, base + 4)
                dve.tensor_tensor(qkv[:, 2 * i + 1, :], tmp[:, 2, :], tmp[:, 3, :], ALU.add).then_inc(rope_step, 1)

            def update(l, hd, b):
                H = l * HEADS + hd
                for d in range(2):
                    pos = A_U + 2 * b + d
                    dve.wait_ge(aux_done, H * AUX_HEAD + (pos + 1))
                    st = state[b % RING][:, d, :]
                    dve.scalar_tensor_tensor(out=st, in0=st, scalar=con[:, ds(hd + C_CD, 1)], in1=aux[pos % 3][:, :],
                                             op0=ALU.mult, op1=ALU.add).then_inc(dve_aux, 1)

            def centre(l, hd):
                H = l * HEADS + hd
                dve.wait_ge(aux_done, H * AUX_HEAD + (A_MEAN + 1))
                mean = aux[A_MEAN % 3][:, 0:T].rearrange("p (o t) -> p o t", o=1).to_broadcast([P, 4, T])
                dve.tensor_tensor(oT[:, :, :], oT[:, :, :], mean, ALU.subtract).then_inc(dve_aux, 1)

            def normalise(l, hd, last=False):
                H = l * HEADS + hd
                dve.wait_ge(rope_step, (H + (1 if last else 2)) * ROPES)
                dve.wait_ge(dve_aux, H * AUX_DVE + 20)
                dve.wait_ge(rstd_done, l * RSTDS + (hd + (RS_RET + 1)))
                for e in range(4):
                    dve.scalar_tensor_tensor(out=tmp[:, e, :], in0=oT[:, e, :], scalar=par[:, ds(hd * 4 + (G_RET + e), 1)],
                                             in1=rstd[:, :], op0=ALU.mult, op1=ALU.mult).then_inc(ret_norm, 1)
                dve.wait_ge(ret_norm, H * 6 + 4)
                dve.wait_ge(sg_ready, H * 4 + 4)
                for e in range(0, 4, 2):
                    dve.tensor_tensor(go[:, ds(hd * 4 + e, 2), :], tmp[:, e:e + 2, :], sg[:, e:e + 2, :], ALU.mult).then_inc(ret_norm, 1)

            def gates(l, hd, first):
                H = l * HEADS + hd
                if not first:
                    dve.wait_ge(ret_norm, H * 6)
                for j in range(4):
                    dve.wait_ge(sig_done, l * SIGS + hd * 4 + (SIG_G + j + 1))
                    dve.tensor_tensor(sg[:, j, :], bank[j][:, 0:T], sig[:, j, :], ALU.mult).then_inc(sg_ready, 1)

            def early(l, hd, first):
                H = l * HEADS + hd
                dve.wait_ge(rope_step, H * ROPES + ROPES)
                if not first:
                    dve.wait_ge(stat_done, l * STATS + (hd + ST_X))
                dve.tensor_tensor(qd[:, :, :], qkv[:, 0:2, SEQ:T],
                                  con[:, ds(hd * 64 + C_QDEC, 64)].rearrange("p (o t) -> p o t", o=1).to_broadcast([P, 2, 64]),
                                  ALU.mult).then_inc(qd_ready, 1)
                dve.wait_ge(aux_done, H * AUX_HEAD + (A_KT + 1))
                dec = con[:, ds(hd * 2 + C_KDEC, 2)].rearrange("p (c o) -> p c o", o=1).to_broadcast([P, 2, DK])
                dve.tensor_tensor(kdec[:, :, :], aux[0][:, :].rearrange("p (c d) -> p c d", c=2), dec, ALU.mult).then_inc(dve_aux, 1)
                dve.wait_ge(aux_done, H * AUX_HEAD + (A_KTS + 1))
                dec = con[0:64, ds(hd * DB + C_KMASK, DB)].rearrange("p (b o) -> p b o", o=1).to_broadcast([64, DB, DK])
                src = aux[1][0:64, 0:DK].rearrange("p (o d) -> p o d", o=1).to_broadcast([64, DB, DK])
                dve.tensor_tensor(kdecs[0:64, :, :], src, dec, ALU.mult).then_inc(dve_aux, 1)
                dve.wait_ge(aux_done, H * AUX_HEAD + (A_S + 1))
                b = aux[A_S % 3]
                dve.tensor_tensor(stm[0:64, SEQ + P:MASKW], b[0:64, SEQ + P:MASKW], con[0:64, ds(hd * MASKW + (C_MASK + SEQ + P), 64)],
                                  ALU.mult).then_inc(stm_half, 1)
                dve.tensor_tensor(stm[:, 0:SEQ + P], b[:, 0:SEQ + P], con[:, ds(hd * MASKW + C_MASK, SEQ + P)], ALU.mult).then_inc(dve_aux, 1)

            def head(l, hd, first):
                prev = hd - 1
                if not first:
                    update(l, prev, 0)
                    update(l, prev, 1)
                    conv_taps(l, hd, 0, 3)
                else:
                    conv_taps(l, hd, 0, 6)
                rope(l, hd, 0, first)
                if not first:
                    update(l, prev, 2)
                    update(l, prev, 3)
                    conv_taps(l, hd, 3, 6)
                    update(l, prev, 4)
                    update(l, prev, 5)
                rope(l, hd, 1, first)
                if not first:
                    update(l, prev, 6)
                    update(l, prev, 7)
                    conv_taps(l, hd, 6, 12)
                    centre(l, prev)
                    conv_taps(l, hd, 12, 20)
                    normalise(l, prev)
                else:
                    conv_taps(l, hd, 6, 20)
                conv_taps(l, hd, 20, TAPS)
                gates(l, hd, first)
                early(l, hd, first)

            stm_half = sem("stm_half")

            dve.memset(ones_d[:, :], 1.0 / D).then_inc(memset_done, 1)
            dve.memset(ones_v[:, :], 1.0 / DV).then_inc(memset_done, 1)
            dve.memset(eps[:, :], EPS).then_inc(memset_done, 1)
            dve.memset(up[:, :, 0:PAD], 0.0).then_inc(memset_done, 1)
            dve.wait_ge(in_loaded, 48)
            with dve.Fori(0, DEPTH) as l:
                dve.tensor_copy(par[:, :], par_all[:, ds(l, 1), :].rearrange("p o c -> p (o c)")).then_inc(par_ready, 1)
                dve.wait_ge(par_ready, l + 1)
                dve.wait_ge(rstd_done, l * RSTDS + 1)
                for k in range(KT):
                    dve.scalar_tensor_tensor(out=h[:, k, :], in0=x[:, k, :], scalar=g_(G_MIXPRE + k), in1=rstd[:, :],
                                             op0=ALU.mult, op1=ALU.mult).then_inc(h_ready, 1)
                dve.wait_ge(u_loaded, l * 16 + 16)
                dve.wait_ge(memset_done, 4)
                for n in range(KT):
                    dve.wait_ge(unit_done, l * UNITS + (U_CIN + 2 * n + 2))
                    dve.wait_ge(sig_done, l * SIGS + (n + 1))
                    b, s = bank[(2 * n + 1) % 4], sig[:, n % 4, :]
                    dve.tensor_tensor(up[:, n, PAD:PAD + SEQ], b[:, 0:SEQ], s[:, 0:SEQ], ALU.mult).then_inc(u_ready, 1)
                    dve.tensor_tensor(us[:, n, :, PAD:PAD + DS], b[:, SEQ:T].rearrange("p (b t) -> p b t", b=DB),
                                      s[:, SEQ:T].rearrange("p (b t) -> p b t", b=DB), ALU.mult).then_inc(u_ready, 1)
                dve.wait_ge(u_ready, l * 16 + 16)
                head(l, 0, True)
                with dve.Fori(1, HEADS) as hd:
                    head(l, hd, False)
                last = HEADS - 1
                for b in range(DB):
                    update(l, last, b)
                centre(l, last)
                normalise(l, last, True)
                for n in range(KT):
                    dve.wait_ge(sig_done, l * SIGS + (SIG_GA + n + 1))
                    dve.wait_ge(unit_done, l * UNITS + (U_RET + 3 * n + 3))
                    if n == 0:
                        pass
                    dve.tensor_tensor(acc2[:, n, :], bank[(2 * n + 1) % 4][:, 0:T], sig[:, n % 4, :], ALU.mult).then_inc(ret_gated, 1)
                    if n == 2:
                        dve.wait_ge(stat_read, l * STATS + (ST_CMEAN + 1))
                        dve.wait_ge(conv_step, l * (KT * CONVS) + KT * CONVS)
                        for k in range(KT):
                            dve.tensor_tensor(acc[:, k, :], acc[:, k, :], cmean[:, :], ALU.subtract).then_inc(conv_norm, 1)
                    if n == 5:
                        dve.wait_ge(conv_norm, l * 24 + 8)
                        dve.wait_ge(rstd_done, l * RSTDS + (RS_CONV + 1))
                        for k in range(KT):
                            dve.scalar_tensor_tensor(out=zt[:, k, :], in0=acc[:, k, :], scalar=g_(G_LNG + k), in1=rstd[:, :],
                                                     op0=ALU.mult, op1=ALU.mult).then_inc(conv_norm, 1)
                for k in range(KT):
                    dve.wait_ge(zsig_done, l * 8 + (k + 1))
                    dve.wait_ge(conv_norm, l * 24 + (8 + k + 1))
                    dve.scalar_tensor_tensor(out=zt[:, k, :], in0=zt[:, k, :], scalar=g_(G_LNB + k), in1=sig[:, k % 4, :],
                                             op0=ALU.add, op1=ALU.mult).then_inc(conv_norm, 1)
                dve.wait_ge(ret_norm, l * (HEADS * 6) + HEADS * 6)
                for n in range(KT):
                    dve.wait_ge(unit_done, l * UNITS + (U_CO + n + 1))
                    dve.wait_ge(sig_done, l * SIGS + (SIG_GB + n + 1))
                    dve.tensor_tensor(tmp[:, n % 4, :], bank[n % 4][:, 0:T], sgb[:, n, :], ALU.mult).then_inc(merge_step, 1)
                    dve.wait_ge(merge_step, l * 16 + (2 * n + 1))
                    dve.wait_ge(ret_gated, l * 8 + (n + 1))
                    dve.tensor_tensor(h[:, n, :], acc2[:, n, :], tmp[:, n % 4, :], ALU.add).then_inc(merge_step, 1)

                def post(sub, rs, sq0, gain, u0, ustep):
                    for n in range(KT):
                        dve.wait_ge(sq_done, l * SQS + (sq0 + n + 1))
                        dve.tensor_copy(acc[:, n, :], bank[n % 4][:, 0:T]).then_inc(y_copied, 1)
                    dve.wait_ge(rstd_done, l * RSTDS + (rs + 1))
                    dve.wait_ge(y_copied, l * 16 + (8 * sub + 8))
                    base = l * 32 + 16 * sub
                    for n in range(KT):
                        dve.scalar_tensor_tensor(out=tmp[:, n % 4, :], in0=acc[:, n, :], scalar=g_(gain + n), in1=rstd[:, :],
                                                 op0=ALU.mult, op1=ALU.mult).then_inc(post_step, 1)
                        dve.wait_ge(post_step, base + (2 * n + 1))
                        dve.tensor_tensor(x[:, n, :], x[:, n, :], tmp[:, n % 4, :], ALU.add).then_inc(post_step, 1)

                post(0, RS_POST, SQ_POST, G_MIXPOST, U_WO, 1)
                dve.wait_ge(post_step, l * 32 + 16)
                dve.wait_ge(rstd_done, l * RSTDS + (RS_FFN + 1))
                for k in range(KT):
                    dve.scalar_tensor_tensor(out=h[:, k, :], in0=x[:, k, :], scalar=g_(G_FFNPRE + k), in1=rstd[:, :],
                                             op0=ALU.mult, op1=ALU.mult).then_inc(h_ready, 1)
                for n in range(FT):
                    b = (2 * n) % 4
                    dve.wait_ge(sig_done, l * SIGS + (SIG_GATE + n + 1))
                    dve.tensor_tensor(tmp[:, n % 4, :], bank[b][:, 0:T], sig[:, n % 4, :], ALU.mult).then_inc(ffn_step, 1)
                    dve.wait_ge(ffn_step, l * (2 * FT) + (2 * n + 1))
                    dve.wait_ge(unit_done, l * UNITS + (U_GU + 2 * n + 2))
                    dve.tensor_tensor(f[:, n, :], bank[b + 1][:, 0:T], tmp[:, n % 4, :], ALU.mult).then_inc(ffn_step, 1)
                post(1, RS_POST2, SQ_POST2, G_FFNPOST, U_DOWN, 3)
                dve.wait_ge(post_step, l * 32 + 32)
                dve.wait_ge(u_saved, l * 32 + 32)


def constants():
    c = np.zeros((P, NCONST), np.float32)
    half = DK // 2
    freqs = (np.float32(10000.0) ** (-np.arange(half, dtype=np.float32) / np.float32(half))).astype(np.float32)
    pos = np.concatenate([np.arange(SEQ), np.tile(PAST + np.arange(DS), DB)]).astype(np.float32)
    ang = (pos[None, :] * freqs[:, None]).astype(np.float32).astype(np.float64)
    c[:, C_COS:C_COS + T], c[:, C_SIN:C_SIN + T] = np.cos(ang), np.sin(ang)
    scale = DK ** -0.5
    p = np.arange(P)
    for h in range(HEADS):
        g = float(np.log1p(-np.exp2(-5.0 - h)))
        j, i = p[:, None], np.arange(SEQ)[None, :]
        m = np.where(i >= j, np.exp(g * np.maximum(i - j, 0)), 0.0) * scale
        o = C_MASK + h * MASKW
        c[:, o:o + SEQ], c[:, o + SEQ:o + SEQ + P] = m, m[:, :P]
        j, i = p[:64, None], p[None, :64]
        c[:64, o + SEQ + P:o + MASKW] = np.where((i // DS == j // DS) & (i >= j), np.exp(g * np.maximum(i - j, 0)), 0.0) * scale
        c[:, C_KDEC + 2 * h] = np.exp(g * (SEQ - 1 - p)) * scale
        c[:, C_KDEC + 2 * h + 1] = np.exp(g * (P - 1 - p)) * scale
        c[:64, C_KMASK + DB * h:C_KMASK + DB * (h + 1)] = (p[:64, None] // DS == np.arange(DB)) * np.exp(g * (DS - 1 - p[:64, None] % DS)) * scale
        c[:, C_QDEC + 64 * h:C_QDEC + 64 * (h + 1)] = np.exp(g * (p[:64] % DS + 1.0))
        c[:, C_CD + h] = math.exp(g * DS)
    c[:, C_ID:C_ID + P] = np.eye(P)
    return c


def units_of(w_in, w_ret_out, w_conv_out, w_o, w_gate, w_up, w_down):
    def tiles(w):
        k, n = w.shape
        t = w.reshape(k // P, P, n // P, P).transpose(2, 1, 0, 3)
        if k // P % UB:
            pad = np.zeros((n // P, P, -(k // P) % UB, P), w.dtype)
            t = np.concatenate([t, pad], axis=2)
        return t.reshape(n // P, P, -1, UB, P).transpose(0, 2, 1, 3, 4)

    win = tiles(w_in)
    q, k, v, g, ca, cb, ga, gb = (win[a // P:b // P] for a, b in zip(
        (0, 1024, 2048, 4096, 6144, 7168, 8192, 9216), (1024, 2048, 4096, 6144, 7168, 8192, 9216, 10240)))
    out = []
    for n in range(KT):
        out += [cb[n], ca[n]]
    for h in range(HEADS):
        out += [*q[2 * h:2 * h + 2], *k[2 * h:2 * h + 2], *v[4 * h:4 * h + 4], *g[4 * h:4 * h + 4]]
    out += list(gb)
    ret = tiles(w_ret_out)
    for n in range(KT):
        out += [ga[n], ret[n]]
    out += [*tiles(w_conv_out), *tiles(w_o)]
    gate, upw = tiles(w_gate), tiles(w_up)
    for n in range(FT):
        out += [gate[n], upw[n]]
    out += list(tiles(w_down))
    return np.concatenate(out)


def kernel(x_prompt, x_sample, state_ret, state_conv, g_mix_pre, g_mix_post, g_ffn_pre, g_ffn_post, w_in, b_gate,
           ret_gn_gain, w_ret_out, conv_w, conv_b, conv_ln_g, conv_ln_b, w_conv_out, w_o, w_ffn_gate, w_ffn_up, w_ffn_down):
    import concourse.bacc as bacc
    from concourse.bass_utils import run_bass_kernel_spmd

    a = {k: np.asarray(v) for k, v in locals().items() if k not in ("bacc", "run_bass_kernel_spmd")}
    feat = lambda v: v.reshape(DEPTH, -1, P).transpose(2, 0, 1)
    x = np.concatenate([a["x_prompt"][0], a["x_sample"].reshape(DB * DS, D)])
    params = np.concatenate(
        [feat(a[k]) for k in ("g_mix_pre", "g_mix_post", "g_ffn_pre", "g_ffn_post", "b_gate", "ret_gn_gain", "conv_b", "conv_ln_g", "conv_ln_b")]
        + [a["conv_w"].reshape(DEPTH, TAPS, KT, P).transpose(3, 0, 2, 1).reshape(P, DEPTH, -1)], axis=2)
    c_in = np.zeros((DEPTH, P, KT, DB, DS + PAD), np.float32)
    c_in[..., 0:PAD] = a["state_conv"].reshape(DEPTH, DB, PAD, KT, P).transpose(0, 4, 3, 1, 2)
    arrays = {
        "w": np.stack([units_of(*(a[k][l] for k in ("w_in", "w_ret_out", "w_conv_out", "w_o", "w_ffn_gate", "w_ffn_up", "w_ffn_down")))
                       for l in range(DEPTH)]).reshape(DEPTH * UNITS, P, UB, P),
        "xin": x.T.reshape(KT, P, T).transpose(1, 0, 2),
        "consts": constants(),
        "params": params,
        "r_in": a["state_ret"].transpose(0, 2, 1, 3, 4).reshape(DEPTH * HEADS * DB, 2, P, DV).transpose(0, 2, 1, 3),
        "c_in": c_in,
    }
    arrays = {k: np.ascontiguousarray(v) for k, v in arrays.items()}
    outs = {
        "x_out": (P, KT, T), "rp_out": (DEPTH * HEADS, P, 2, DV), "rs_out": (DEPTH * HEADS * DB, P, 2, DV),
        "cp_out": (DEPTH, P, KT, SEQ + PAD), "cs_out": (DEPTH, P, KT, DB, DS + PAD),
    }
    nc = bacc.Bacc("TRN2", target_bir_lowering=False, num_devices=1, dynamic_dma_scratch_size=4096)
    args = [nc.dram_tensor(k, v.shape, F32, kind="ExternalInput").ap() for k, v in arrays.items()]
    args += [nc.dram_tensor(k, s, F32, kind="ExternalOutput").ap() for k, s in outs.items()]
    program(nc, *args)
    r = run_bass_kernel_spmd(nc, [arrays], core_ids=[0]).results[0]
    y = r["x_out"].transpose(1, 0, 2).reshape(D, T).T
    rp = r["rp_out"].reshape(DEPTH, 1, HEADS, P, 2, DV).transpose(0, 1, 2, 4, 3, 5).reshape(DEPTH, 1, HEADS, DK, DV)
    rs = r["rs_out"].reshape(DEPTH, HEADS, DB, P, 2, DV).transpose(0, 2, 1, 4, 3, 5).reshape(DEPTH, DB, HEADS, DK, DV)
    cp = r["cp_out"][..., SEQ:].transpose(0, 3, 2, 1).reshape(DEPTH, 1, PAD, D)
    cs = r["cs_out"][..., DS:].transpose(0, 3, 4, 2, 1).reshape(DEPTH, DB, PAD, D)
    return tuple(np.ascontiguousarray(v) for v in (y[:SEQ].reshape(1, SEQ, D), y[SEQ:].reshape(DB, DS, D), rp, cp, rs, cs))
```

```python
import math
from contextlib import ExitStack

import numpy as np

import concourse.bass as bass
from concourse import mybir

F32 = mybir.dt.float32
F32R = mybir.dt.float32r
ALU = mybir.AluOpType
ACT = mybir.ActivationFunctionType
ds = bass.ds

P = 128
D = 1024
DEPTH = 2
SEQ = 256
DB, DS = 8, 8
PAST = 2048
T = SEQ + DB * DS
HEADS = 4
DK, DV = 256, 512
TAPS = 31
PAD = TAPS - 1
FF = 2816
EPS = 1e-6
KT = D // P
FT = FF // P
VT = HEADS * DV // P
UB = 8
RING = 4
SBUF_END = 229344
AHEAD = 3

U_CIN, U_HEAD, U_GB, U_RET, U_CO, U_WO, U_GU, U_DOWN, UNITS = 0, 16, 64, 72, 96, 104, 112, 156, 180
HEAD_UNITS = 12
SIGS, SIG_G, SIG_GB, SIG_GA, SIG_GATE = 62, 8, 24, 32, 40
SQS, SQ_RET, SQ_CONV, SQ_POST, SQ_FFN, SQ_POST2 = 44, 8, 12, 20, 28, 36
STATS, ST_X, ST_CMEAN, ST_CVAR, ST_POST, ST_FFN, ST_POST2 = 10, 1, 5, 6, 7, 8, 9
RSTDS, RS_RET, RS_CONV, RS_POST, RS_FFN, RS_POST2 = 9, 1, 5, 6, 7, 8
AUX_HEAD, AUX_ACT, AUX_DVE = 28, 8, 20
ROPES, CONVS, POSTS = 12, TAPS, 16
LATE_TAPS = 5

A_KT, A_KTS, A_S, A_V, A_P, A_U, A_PU, A_MEAN, A_VAR = 0, 1, 2, 3, 6, 8, 24, 26, 27
READER = ([("dve", 0), ("act", 0), ("dve", 1), ("act", 1), ("act", 2), ("dve", 2), ("act", 3), ("act", 4)]
          + [("dve", 3 + i) for i in range(16)] + [("act", 5), ("act", 6), ("dve", 19), ("act", 7)])
BEFORE = {0: 27, 1: 25, 2: 26}

C_COS, C_SIN, C_MASK, C_KDEC, C_KROW, C_OWN, C_QDEC, C_CD, C_ID = 0, 320, 640, 2432, 2440, 2444, 2452, 2708, 2712
NCONST = C_ID + P
MASKW = 448
G_MIXPRE, G_MIXPOST, G_FFNPRE, G_FFNPOST, G_GATE, G_RET, G_CB, G_LNG, G_LNB, G_CW = 0, 8, 16, 24, 32, 48, 64, 72, 80, 88
NPAR = G_CW + KT * TAPS


def program(nc, w, xin, consts, params, r_in, c_in, x_out, rp_out, rs_out, cp_out, cs_out):
    ctx = ExitStack()
    with ctx:
        def sem(name):
            return ctx.enter_context(nc.semaphore(name))

        at = [-(-nc.sbuf_base // 32) * 32]

        def sb(name, *shape, dtype=F32, offset=None):
            where = at[0] if offset is None else offset
            if offset is None:
                at[0] += -(-4 * math.prod(shape) // 32) * 32
            return nc.alloc_sbuf_tensor_at(name, [P, *shape], dtype, offset=where)

        wring = [sb(f"wring{i}", UB, P) for i in range(RING)]
        whi = [sb(f"whi{i}", UB, P, dtype=F32R) for i in range(RING)]
        wlo = [sb(f"wlo{i}", UB, P, dtype=F32R) for i in range(RING)]
        x = sb("x", KT, T)
        hhi, hlo = sb("hhi", KT, T, dtype=F32R), sb("hlo", KT, T, dtype=F32R)
        acc = sb("acc", KT, T)
        rstd = sb("rstd", T)
        lnv = sb("lnv", T)
        cmean = lnv
        sig = sb("sig", 4, T)
        tmp = sb("tmp", 4, T)
        con = sb("con", NCONST)
        par = sb("par", NPAR)
        ones_d = sb("ones_d", P)
        ones_v = sb("ones_v", P)
        eps = sb("eps", 1)
        qkv_at = at[0]
        qkv = sb("qkv", 8, T)
        sgb = sb("sgb", KT, T, offset=qkv_at)
        sq8 = sb("sq8", KT, T, offset=qkv_at)
        go_at = at[0]
        go = sb("go", VT, T)
        zhi = sb("zhi", KT, T, dtype=F32R, offset=go_at)
        zlo = sb("zlo", KT, T, dtype=F32R, offset=go_at + KT * T * 4)
        sqz = sb("sqz", KT, T, offset=go_at + KT * T * 4)
        up_at = at[0]
        up = sb("up", KT, SEQ + PAD)
        us = sb("us", KT, DB, DS + PAD)
        stap = sb("stap", KT, DB, DS, offset=go_at + (HEADS - 1) * 4 * T * 4)
        acc2 = sb("acc2", KT, T, offset=up_at)
        head_at = at[0]
        kdec = sb("kdec", 2, DK)
        kdecs = sb("kdecs", DB, DK, dtype=F32R)
        vtok = sb("vtok", 3, DV)
        vshi, vslo = sb("vshi", DV, dtype=F32R), sb("vslo", DV, dtype=F32R)
        stm = sb("stm", MASKW)
        qd = sb("qd", 2, DB * DS)
        pst = sb("pst", 2, DV)
        state = [sb(f"state{i}", 2, DV) for i in range(RING)]
        sg = sb("sg", 4, T)
        oT = sb("oT", 4, T)
        sqo_at = at[0]
        sqo = sb("sqo", 4, T)
        kdup = sb("kdup", 2, P, offset=sqo_at)
        vdup = sb("vdup", 4, P, offset=sqo_at + 8 * P)
        kd = sb("kd", DK, offset=sqo_at + 24 * P)
        khl = sb("khl", DK, dtype=F32R, offset=sqo_at + 32 * P)
        ghi = sb("ghi", VT, T, dtype=F32R, offset=head_at)
        glo = sb("glo", VT, T, dtype=F32R, offset=head_at + VT * T * 4)
        fhi = sb("fhi", FT, T, dtype=F32R, offset=go_at)
        flo = sb("flo", FT, T, dtype=F32R, offset=go_at + FT * T * 4)
        assert at[0] <= SBUF_END, at[0] - SBUF_END
        assert head_at + 2 * VT * T * 4 <= at[0] and go_at + 2 * FT * T * 4 <= at[0]

        bank = [ctx.enter_context(nc.psum_tensor(f"bank{i}", [P, 512], F32)) for i in range(8)]
        aux = bank[4:7]
        X = bank[7]

        w_ready = [sem(f"w_ready{i}") for i in range(RING)]
        hi_done = sem("hi_done")
        lo_done = sem("lo_done")
        unit_done = sem("unit_done")
        aux_done = sem("aux_done")
        stat_done = sem("stat_done")
        sig_done = sem("sig_done")
        v_copied = sem("v_copied")
        sq_done = sem("sq_done")
        stat_read = sem("stat_read")
        rstd_done = sem("rstd_done")
        act_aux = sem("act_aux")
        zsig_done = sem("zsig_done")
        dve_aux = sem("dve_aux")
        memset_done = sem("memset_done")
        log_loaded = sem("log_loaded")
        pad_zeroed = sem("pad_zeroed")
        h_value, h_hi, h_ready = sem("h_value"), sem("h_hi"), sem("h_ready")
        dup_ready, kd_ready, khl_step, ks_ready = sem("dup_ready"), sem("kd_ready"), sem("khl_step"), sem("ks_ready")
        vs_hi = sem("vs_hi")
        g_hi, g_ready = sem("g_hi"), sem("g_ready")
        z_hi, z_ready = sem("z_hi"), sem("z_ready")
        m_hi, m_ready = sem("m_hi"), sem("m_ready")
        f_hi, f_ready = sem("f_hi"), sem("f_ready")
        u_ready = sem("u_ready")
        rope_step = sem("rope_step")
        qd_ready = sem("qd_ready")
        sample_masked = sem("sample_masked")
        sg_ready = sem("sg_ready")
        ret_norm = sem("ret_norm")
        conv_step, sample_conv_step = sem("conv_step"), sem("sample_conv_step")
        conv_norm = sem("conv_norm")
        ret_gated = sem("ret_gated")
        merge_step = sem("merge_step")
        y_copied = sem("y_copied")
        post_step = sem("post_step")
        ffn_step = sem("ffn_step")
        x_loaded, par_loaded, con_loaded = sem("x_loaded"), sem("par_loaded"), sem("con_loaded")
        u_loaded = sem("u_loaded")
        u_saved = sem("u_saved")
        r_loaded = [sem(f"r_loaded{i}") for i in range(RING)]
        r_stored = [sem(f"r_stored{i}") for i in range(RING)]
        pst_stored = sem("pst_stored")
        x_stored = sem("x_stored")

        def col(c0, n):
            return con[:, c0:c0 + n]

        def g_(c):
            return par[:, c:c + 1]

        block = ctx.enter_context(nc.Block())

        @block.sync
        def _(sp):
            sp.dma_start(x[:, :, :], xin).then_inc(x_loaded, 16)
            for s in range(RING):
                sp.dma_start(wring[s][:, :, :], w[s]).then_inc(w_ready[s], 16)
            with sp.Fori(1, DEPTH * UNITS // RING + 1) as i:
                for s in range(RING):
                    sp.wait_ge(lo_done, i * RING + (s + 1 - RING))
                    sp.dma_start(wring[s][:, :, :], w[i * RING + s]).then_inc(w_ready[s], 16)
            for s in range(RING):
                sp.wait_ge(w_ready[s], (DEPTH * UNITS // RING + 1) * 16)

        @block.gpsimd
        def _(pool):
            def load(l, j, s):
                pool.dma_start(state[s][:, :, :], r_in[l * (HEADS * DB) + j]).then_inc(r_loaded[s], 16)

            def sample_conv_tap(l, k, first=False):
                out = acc[:, :, SEQ:T].rearrange("p n (b t) -> p n b t", b=DB)
                weights = par[:, G_CW:G_CW + KT * TAPS].rearrange("p (n k) -> p n k", n=KT)
                tap = weights[:, :, ds(k, 1)].rearrange("p n (b t) -> p n b t", b=1).to_broadcast([P, KT, DB, DS])
                bias = par[:, G_CB:G_CB + KT].rearrange("p (n b t) -> p n b t", b=1, t=1).to_broadcast([P, KT, DB, DS])
                if not first:
                    pool.wait_ge(sample_conv_step, l * (2 * TAPS) + 2 * k)
                pool.tensor_tensor(out if first else stap[:, :, :, :], us[:, :, :, ds(k, DS)], tap, ALU.mult).then_inc(sample_conv_step, 1)
                pool.wait_ge(sample_conv_step, l * (2 * TAPS) + 2 * k + 1)
                pool.tensor_tensor(out, out, bias if first else stap[:, :, :, :], ALU.add).then_inc(sample_conv_step, 1)

            def head(l, hd, last):
                for b in range(DB):
                    pool.wait_ge(dve_aux, (l * HEADS + hd) * AUX_DVE + (3 + 2 * b + 2))
                    s = b % RING
                    pool.dma_start(rs_out[(l * HEADS + hd) * DB + b], state[s][:, :, :]).then_inc(r_stored[s], 16)
                    if b and not (last and b > RING):
                        pool.wait_ge(r_stored[(b - 1) % RING], (l * HEADS + hd) * 32 + 16 * ((b - 1) // RING + 1))
                        load(l, hd * DB + (b - 1 + RING), (b - 1) % RING)
                if not last:
                    pool.wait_ge(r_stored[RING - 1], (l * HEADS + hd) * 32 + 32)
                    load(l, hd * DB + (DB - 1 + RING), RING - 1)
                if not last:
                    for i in range(LATE_TAPS):
                        sample_conv_tap(l, hd * LATE_TAPS + (TAPS - (HEADS - 1) * LATE_TAPS + i))
                pool.wait_ge(act_aux, (l * HEADS + hd) * AUX_ACT + 7)
                pool.dma_start(rp_out[l * HEADS + hd], pst[:, :, :]).then_inc(pst_stored, 16)

            pool.dma_start(par[:, :], params[0]).then_inc(par_loaded, 16)
            pool.wait_ge(w_ready[1], 16)
            pool.dma_start(con[:, :], consts).then_inc(con_loaded, 16)
            with pool.Fori(0, DEPTH) as l:
                pool.dma_start(us[:, :, :, :], c_in[l]).then_inc(u_loaded, 16)
                for s in range(RING):
                    load(l, s, s)
                pool.wait_ge(u_ready, l * 16 + 16)
                pool.dma_start(cp_out[l], up[:, :, :]).then_inc(u_saved, 16)
                pool.dma_start(cs_out[l], us[:, :, :, :]).then_inc(u_saved, 16)
                for k in range(TAPS - (HEADS - 1) * LATE_TAPS):
                    sample_conv_tap(l, k, k == 0)
                with pool.Fori(0, HEADS - 1) as hd:
                    head(l, hd, False)
                head(l, HEADS - 1, True)
                pool.wait_ge(u_saved, l * 32 + 32)
                pool.wait_ge(sample_conv_step, l * (2 * TAPS) + 2 * TAPS)
                for s in range(RING):
                    pool.wait_ge(r_stored[s], l * (HEADS * 32) + HEADS * 32)
                pool.wait_ge(unit_done, l * UNITS + UNITS)
                pool.wait_ge(y_copied, l * 16 + 16)
                pool.dma_start(par[:, :], params[l + 1]).then_inc(par_loaded, 16)
            pool.wait_ge(post_step, DEPTH * POSTS)
            pool.dma_start(x_out, x[:, :, :]).then_inc(x_stored, 16)
            pool.wait_ge(x_stored, 16)
            pool.wait_ge(par_loaded, (DEPTH + 1) * 16)
            pool.wait_ge(pst_stored, DEPTH * HEADS * 16)

        @block.tensor
        def _(pe):
            def unit(l, q, j, g, rhs, k0=0, n=UB, start=True, stop=True, ready=None, between=None):
                pe.wait_ge(lo_done, l * UNITS + q * RING + (j + 1))
                for k in range(n):
                    if ready is not None:
                        ready(k0 + k)
                    hi, lo = rhs(k0 + k)
                    pe.matmul(bank[g][:, 0:T], whi[j][:, k, :], hi, start=start and k == 0, stop=False)
                    pe.matmul(bank[g][:, 0:T], whi[j][:, k, :], lo, start=False, stop=False)
                    mm = pe.matmul(bank[g][:, 0:T], wlo[j][:, k, :], hi, start=False, stop=stop and k == n - 1)
                    if k == n - 1:
                        mm.then_inc(unit_done, 1)
                    if between is not None:
                        between(k)

            def tile_of(hi, lo):
                return lambda k: (hi[:, k, :], lo[:, k, :])

            h_tile = tile_of(hhi, hlo)

            def stat(l, i, src, n, ones, sq=None, out=X):
                for k in range(n):
                    if sq is not None:
                        sq(k)
                    mm = pe.matmul(out[:, 0:T], ones[:, :], src(k), start=(k == 0), stop=(k == n - 1))
                return mm

            def aux_free(H, pos, first=False):
                if pos >= 3:
                    who, n = READER[pos - 3]
                elif first:
                    return
                else:
                    who, n = READER[BEFORE[pos]]
                    H = H - 1
                if who == "act":
                    pe.wait_ge(act_aux, H * AUX_ACT + (n + 1))
                else:
                    pe.wait_ge(dve_aux, H * AUX_DVE + (n + 1))

            def early(l, hd, j, first=False):
                H = l * HEADS + hd
                ident = con[:, C_ID:C_ID + P]

                def value_rows(c):
                    for e in range(4):
                        src = qkv[:, 4 + e, c * P:(c + 1) * P] if c < 2 else vdup[:, e, :]
                        mm = pe.transpose(aux[(A_V + c) % 3][:, e * P:(e + 1) * P], src, ident)
                    mm.then_inc(aux_done, 1)

                if j == 8:
                    aux_free(H, A_KT, first)
                    aux_free(H, A_KTS, first)
                    pe.wait_ge(rope_step, H * ROPES + ROPES)
                    for c in range(2):
                        for d in range(2):
                            mm = pe.transpose(aux[0][:, c * DK + d * P:c * DK + (d + 1) * P], qkv[:, 2 + d, c * P:(c + 1) * P], ident)
                    mm.then_inc(aux_done, 1)
                    pe.wait_ge(dup_ready, H * 2 + 1)
                    for d in range(2):
                        mm = pe.transpose(aux[1][:, d * P:(d + 1) * P], kdup[:, d, :], ident)
                    mm.then_inc(aux_done, 1)
                if j == 9:
                    aux_free(H, A_S, first)
                    b = aux[A_S % 3]
                    for o, j0, n, i0, m in ((0, 0, P, 0, SEQ), (SEQ, P, P, P, P), (SEQ + P, SEQ, 64, SEQ, 64)):
                        for d in range(2):
                            mm = pe.matmul(b[0:n, o:o + m], qkv[:, 2 + d, j0:j0 + n], qkv[:, d, i0:i0 + m],
                                           start=(d == 0), stop=(d == 1))
                    mm.then_inc(aux_done, 1)
                if j == 10:
                    pe.wait_ge(v_copied, H * 4 + 4)
                    for c in range(2):
                        aux_free(H, A_V + c)
                        value_rows(c)
                if j == 11:
                    pe.wait_ge(dup_ready, H * 2 + 2)
                    value_rows(2)

            def late_out(l, hd, p):
                H = l * HEADS + hd
                if p == 0:
                    pe.wait_ge(dve_aux, H * AUX_DVE + 3)
                    pe.wait_ge(act_aux, H * AUX_ACT + 3)
                aux_free(H, A_P + p)
                for i in range(2):
                    e = 2 * p + i
                    o = aux[(A_P + p) % 3]
                    pe.matmul(o[:, i * SEQ:(i + 1) * SEQ], vtok[:, 0, e * P:(e + 1) * P], stm[:, 0:SEQ], start=True, stop=False)
                    mm = pe.matmul(o[:, i * SEQ + P:(i + 1) * SEQ], vtok[:, 1, e * P:(e + 1) * P], stm[:, SEQ:SEQ + P],
                                   start=False, stop=True)
                mm.then_inc(aux_done, 1)

            def late_within(l, hd):
                pe.wait_ge(qd_ready, l * HEADS + hd + 1)
                for e in range(4):
                    pe.matmul(X[:, e * 64:(e + 1) * 64], vtok[0:64, 2, e * P:(e + 1) * P], stm[0:64, SEQ + P:MASKW],
                              start=(e == 0), stop=False, skip_group_check=True)

            def late_state(l, hd, b, d, half):
                H = l * HEADS + hd
                s = b % RING
                if b == 0 and d == 0 and half == 0:
                    pe.wait_ge(ks_ready, H + 1)
                if d == 0 and half == 0:
                    pe.wait_ge(r_loaded[s], H * 32 + (b // RING + 1) * 16)
                for e in (2 * half, 2 * half + 1):
                    mm = pe.matmul(X[:, e * 64 + b * DS:e * 64 + (b + 1) * DS], state[s][:, d, e * P:(e + 1) * P],
                                   qd[:, d, b * DS:(b + 1) * DS], start=False, stop=(d == 1), skip_group_check=True)
                if b == DB - 1 and d == 1 and half == 1:
                    mm.then_inc(stat_done, 1)
                if half == 1:
                    pos = A_U + 2 * b + d
                    aux_free(H, pos)
                    pe.matmul(aux[pos % 3][:, :], kdecs[:, b, d * P:(d + 1) * P], vshi[:, :], start=True, stop=False)
                    pe.matmul(aux[pos % 3][:, :], kdecs[:, b, d * P:(d + 1) * P], vslo[:, :],
                              start=False, stop=True).then_inc(aux_done, 1)

            def late_prompt_state(l, hd, d):
                H = l * HEADS + hd
                pos = A_PU + d
                aux_free(H, pos)
                for c in range(2):
                    mm = pe.matmul(aux[pos % 3][:, :], kdec[:, c, d * P:(d + 1) * P], vtok[:, c, :],
                                   start=(c == 0), stop=(c == 1))
                mm.then_inc(aux_done, 1)

            def late_mean(l, hd):
                H = l * HEADS + hd
                aux_free(H, A_MEAN)
                pe.wait_ge(act_aux, H * AUX_ACT + 5)
                pe.wait_ge(stat_read, l * STATS + (hd + (ST_X + 1)))
                stat(l, 0, lambda k: oT[:, k, :], 4, ones_v, out=aux[A_MEAN % 3]).then_inc(aux_done, 1)

            def late_var(l, hd):
                H = l * HEADS + hd
                aux_free(H, A_VAR)
                pe.wait_ge(sq_done, l * SQS + (hd + (SQ_RET + 1)))
                stat(l, 0, lambda k: sqo[:, k, :], 4, ones_v, out=aux[A_VAR % 3]).then_inc(aux_done, 1)

            def late(l, hd, j, k):
                if j == 0 and k in (4, 6):
                    late_out(l, hd, (k - 4) // 2)
                if j == 0 and k == 7:
                    late_within(l, hd)
                if 1 <= j <= 4:
                    late_state(l, hd, 2 * (j - 1) + k // 4, k % 4 // 2, k % 2)
                if j == 5 and k in (2, 5):
                    late_prompt_state(l, hd, k // 3)
                if j == 5 and k == 7:
                    late_mean(l, hd)
                if j == 7 and k == 7:
                    late_var(l, hd)

            def head(l, hd, first):
                H = l * HEADS + hd
                for j in range(HEAD_UNITS):
                    if j < 4 and first:
                        if j % 2 == 0:
                            pe.wait_ge(sig_done, l * SIGS + (7 + j // 2))
                        else:
                            pe.wait_ge(u_ready, l * 16 + (14 + j - 1))
                    elif j < 4:
                        pe.wait_ge(sg_ready, H * 4 + (j + 1 - 4))
                    elif j < 8:
                        pe.wait_ge(rope_step, H * ROPES + (3, 4, 9, 10)[j - 4])
                    else:
                        pe.wait_ge(v_copied, H * 4 + (j - 7))
                    if j == 11:
                        aux_free(H, A_V + 2)
                    unit(l, hd * 3 + (U_HEAD // RING + j // RING), j % RING, j % 4, h_tile,
                         between=None if first else lambda k: late(l, hd - 1, j, k))
                    early(l, hd, j, first)

            def h_read(l, k):
                pe.wait_ge(h_ready, l * 16 + (k + 1))

            pe.wait_ge(memset_done, 3)
            with pe.Fori(0, DEPTH) as l:
                stat(l, 0, lambda k: sq8[:, k, :], KT, ones_d, lambda k: pe.wait_ge(sq_done, l * SQS + (k + 1))).then_inc(stat_done, 1)
                for j in range(4):
                    unit(l, 0, j, j, h_tile, ready=(lambda k: h_read(l, k)) if j == 0 else None)
                with pe.Fori(1, 4) as i:
                    for j in range(4):
                        if j % 2 == 0:
                            pe.wait_ge(sig_done, l * SIGS + i * 2 + (j // 2 - 1))
                        else:
                            pe.wait_ge(u_ready, l * 16 + i * 4 + (j - 3))
                        unit(l, i, j, j, h_tile)
                pe.wait_ge(con_loaded, 16)
                head(l, 0, True)
                with pe.Fori(1, HEADS) as hd:
                    head(l, hd, False)
                for n in range(KT):
                    if n < 4:
                        pe.wait_ge(sg_ready, l * 16 + (13 + n))
                    else:
                        pe.wait_ge(sig_done, l * SIGS + (SIG_GB + n - 3))
                    u = U_GB + n
                    unit(l, u // RING, u % RING, n % 4, h_tile, between=lambda k: late(l, HEADS - 1, n, k))
                for n in range(KT):
                    g = (2 * n) % 4
                    if n < 2:
                        pe.wait_ge(sig_done, l * SIGS + (SIG_GB + 5 + 2 * n))
                    else:
                        pe.wait_ge(sig_done, l * SIGS + (SIG_GA + n - 1))
                    u = U_RET + 3 * n
                    unit(l, u // RING, u % RING, g, h_tile)
                    if n < 2:
                        pe.wait_ge(sig_done, l * SIGS + (SIG_GB + 6 + 2 * n))
                    else:
                        pe.wait_ge(ret_gated, l * 8 + (n - 1))
                    for p in range(2):
                        u = U_RET + 3 * n + 1 + p
                        unit(l, u // RING, u % RING, g + 1, tile_of(ghi, glo), k0=8 * p, start=(p == 0), stop=(p == 1),
                             ready=(lambda k: pe.wait_ge(g_ready, l * 7 + (k // 4 + 1 if k < 12 else k - 8))) if n == 0 else None)
                    if n == 1:
                        pe.wait_ge(conv_step, l * (KT * CONVS) + KT * CONVS)
                        pe.wait_ge(sample_conv_step, l * (2 * TAPS) + 2 * TAPS)
                        stat(l, 0, lambda k: acc[:, k, :], KT, ones_d).then_inc(stat_done, 1)
                    if n == 4:
                        pe.wait_ge(stat_read, l * STATS + (ST_CMEAN + 1))
                        stat(l, 0, lambda k: sqz[:, k, :], KT, ones_d,
                             lambda k: pe.wait_ge(sq_done, l * SQS + (SQ_CONV + k + 1))).then_inc(stat_done, 1)
                for n in range(KT):
                    if n < 4:
                        if n % 2 == 0:
                            pe.wait_ge(sig_done, l * SIGS + (SIG_GA + 7 + n // 2))
                        else:
                            pe.wait_ge(ret_gated, l * 8 + (7 + n // 2))
                    else:
                        pe.wait_ge(merge_step, l * 16 + (2 * (n - 4) + 1))
                    u = U_CO + n
                    unit(l, u // RING, u % RING, n % 4, tile_of(zhi, zlo),
                         ready=(lambda k: pe.wait_ge(z_ready, l * 8 + (k + 1))) if n == 0 else None)
                for n in range(KT):
                    if n < 4:
                        pe.wait_ge(merge_step, l * 16 + (2 * (n + 4) + 1))
                    else:
                        pe.wait_ge(y_copied, l * 16 + (n - 3))
                    u = U_WO + n
                    unit(l, u // RING, u % RING, n % 4, h_tile,
                         ready=(lambda k: pe.wait_ge(m_ready, l * 8 + (k + 1))) if n == 0 else None)
                pe.wait_ge(stat_read, l * STATS + (ST_CVAR + 1))
                stat(l, 0, lambda k: sq8[:, k, :], KT, ones_d,
                     lambda k: pe.wait_ge(sq_done, l * SQS + (SQ_POST + k + 1))).then_inc(stat_done, 1)
                pe.wait_ge(stat_read, l * STATS + (ST_POST + 1))
                stat(l, 0, lambda k: sq8[:, k, :], KT, ones_d,
                     lambda k: pe.wait_ge(sq_done, l * SQS + (SQ_FFN + k + 1))).then_inc(stat_done, 1)
                for j in range(4):
                    unit(l, U_GU // RING, j, j, h_tile, ready=(lambda k: h_read(l, 8 + k)) if j == 0 else None)
                with pe.Fori(1, FT // 2) as i:
                    for j in range(4):
                        pe.wait_ge(ffn_step, l * (2 * FT) + i * 4 + (j - 3))
                        unit(l, i + U_GU // RING, j, j, h_tile)
                for n in range(KT):
                    if n < 4:
                        pe.wait_ge(ffn_step, l * (2 * FT) + (2 * FT - 3 + n))
                    else:
                        pe.wait_ge(y_copied, l * 16 + (8 + n - 3))
                    for p in range(3):
                        u = U_DOWN + 3 * n + p
                        unit(l, u // RING, u % RING, n % 4, tile_of(fhi, flo), k0=8 * p, n=min(8, FT - 8 * p),
                             start=(p == 0), stop=(p == 2),
                             ready=(lambda k: pe.wait_ge(f_ready, l * FT + (k + 1))) if n == 0 else None)
                pe.wait_ge(stat_read, l * STATS + (ST_FFN + 1))
                stat(l, 0, lambda k: sq8[:, k, :], KT, ones_d,
                     lambda k: pe.wait_ge(sq_done, l * SQS + (SQ_POST2 + k + 1))).then_inc(stat_done, 1)

        @block.scalar
        def _(act):
            def split(l, u):
                v = u + AHEAD
                s = v % RING
                act.wait_ge(w_ready[s], l * (UNITS // RING * 16) + (v // RING + 1) * 16)
                if v >= RING:
                    act.wait_ge(unit_done, l * UNITS + (v + 1 - RING))
                act.activation(whi[s][:, :, :], wring[s][:, :, :], ACT.Copy).then_inc(hi_done, 1)

            def gemm(l, u):
                act.wait_ge(unit_done, l * UNITS + (u + 1))

            def log_table(l, rs):
                if not (isinstance(rs, int) and rs == 0):
                    act.wait_ge(rstd_done, l * RSTDS + rs)
                act.activation(lnv[:, 0:1], eps[:, 0:1], ACT.Ln).then_inc(log_loaded, 1)

            def rsqrt(l, src, st, rs, aux_read=None):
                act.wait_ge(log_loaded, l * RSTDS + rs + 1)
                ln = act.activation(lnv[:, :], src, ACT.Ln, bias=eps[:, 0:1])
                if aux_read is None:
                    ln.then_inc(stat_read, 1)
                    act.wait_ge(stat_read, l * STATS + (st + 1))
                else:
                    ln.then_inc(act_aux, 1)
                    act.wait_ge(act_aux, aux_read)
                act.activation(rstd[:, :], lnv[:, :], ACT.Exp, scale=-0.5).then_inc(rstd_done, 1)

            def split_head(l, hd, j):
                v = j + AHEAD
                s = v % RING
                act.wait_ge(w_ready[s], l * (UNITS // RING * 16) + hd * (HEAD_UNITS // RING * 16) + ((U_HEAD + v) // RING + 1) * 16)
                act.wait_ge(unit_done, l * UNITS + hd * HEAD_UNITS + (U_HEAD + v + 1 - RING))
                act.activation(whi[s][:, :, :], wring[s][:, :, :], ACT.Copy).then_inc(hi_done, 1)

            def sigmoid(dst, src, bias=None):
                if bias is None:
                    act.activation(dst, src, ACT.Sigmoid).then_inc(sig_done, 1)
                else:
                    act.activation(dst, src, ACT.Sigmoid, bias=bias).then_inc(sig_done, 1)

            def late(l, hd, j):
                H = l * HEADS + hd
                if j == 0:
                    for p in range(2):
                        act.wait_ge(aux_done, H * AUX_HEAD + (A_P + p + 1))
                        act.activation(oT[:, 2 * p:2 * p + 2, 0:SEQ], aux[(A_P + p) % 3][:, :].rearrange("p (e t) -> p e t", e=2),
                                       ACT.Copy).then_inc(act_aux, 1)
                if j == 5:
                    act.wait_ge(stat_done, l * STATS + (hd + (ST_X + 1)))
                    act.activation(oT[:, :, SEQ:T], X[:, 0:256].rearrange("p (e t) -> p e t", e=4), ACT.Copy).then_inc(stat_read, 1)
                if j == 5:
                    for d in range(2):
                        act.wait_ge(aux_done, H * AUX_HEAD + (A_PU + d + 1))
                        act.activation(pst[:, d, :], aux[(A_PU + d) % 3][:, :], ACT.Copy).then_inc(act_aux, 1)
                if j == 6:
                    act.wait_ge(dve_aux, H * AUX_DVE + 20)
                    act.activation(sqo[:, :, :], oT[:, :, :], ACT.Square).then_inc(sq_done, 1)
                    log_table(l, hd + RS_RET)
                if j == 8:
                    act.wait_ge(aux_done, H * AUX_HEAD + (A_VAR + 1))
                    rsqrt(l, aux[A_VAR % 3][:, 0:T], None, hd + RS_RET, aux_read=H * AUX_ACT + 8)

            def head(l, hd, first):
                H = l * HEADS + hd
                for j in range(HEAD_UNITS):
                    split_head(l, hd, j)
                    if not first and j < 8:
                        late(l, hd - 1, j)
                    if 4 <= j < 8:
                        if j == 4 and not first:
                            act.wait_ge(aux_done, H * AUX_HEAD + (A_V + 3 - AUX_HEAD))
                        act.wait_ge(unit_done, l * UNITS + hd * HEAD_UNITS + (U_HEAD + j + 1))
                        act.activation(qkv[:, j, :], bank[j % 4][:, 0:T], ACT.Copy).then_inc(v_copied, 1)
                    if j == 8 and not first:
                        late(l, hd - 1, 8)
                    if j == 8:
                        act.wait_ge(rope_step, H * ROPES + ROPES)
                        act.wait_ge(v_copied, H * 4 + 4)
                        for buf, t0, n in ((kdup, 2, 2), (vdup, 4, 4)):
                            src = qkv[:, t0:t0 + n, SEQ:T].rearrange("p d (o t) -> p d o t", o=1).to_broadcast([P, n, 2, T - SEQ])
                            act.activation(buf[:, :, :].rearrange("p d (o t) -> p d o t", o=2), src, ACT.Copy).then_inc(dup_ready, 1)
                    if j == 9:
                        act.wait_ge(aux_done, H * AUX_HEAD + (A_KTS + 1))
                        act.activation(kd[:, :], aux[1][:, 0:DK], ACT.Copy, scale=con[:, ds(hd + C_KROW, 1)]).then_inc(act_aux, 1)
                        act.wait_ge(act_aux, H * AUX_ACT + 1)
                        act.activation(khl[:, :], kd[:, :], ACT.Copy).then_inc(kd_ready, 1)
                    if j >= 8:
                        if first:
                            act.wait_ge(u_ready, l * 16 + (2 * (j - 4) + 2))
                        else:
                            act.wait_ge(sg_ready, H * 4 + (j - 7 - 4))
                        act.wait_ge(unit_done, l * UNITS + hd * HEAD_UNITS + (U_HEAD + j + 1))
                        sigmoid(sig[:, j - 8, :], bank[j % 4][:, 0:T])
                    if j >= 10:
                        for c in ((0, 1), (2,))[j - 10]:
                            n = P if c < 2 else T - SEQ
                            act.wait_ge(aux_done, H * AUX_HEAD + (A_V + c + 1))
                            act.activation(vtok[0:n, c, :], aux[(A_V + c) % 3][0:n, :], ACT.Copy).then_inc(act_aux if c < 2 else vs_hi, 1)
                            if c == 2:
                                act.activation(vshi[:, :], aux[(A_V + c) % 3][:, :], ACT.Copy).then_inc(vs_hi, 1)
                if not first:
                    act.wait_ge(ret_norm, H * 6)
                    act.wait_ge(pst_stored, H * 16)

            def squares_of_products(l, u0, ustep, sq0):
                for n in range(KT):
                    for p in range(ustep):
                        split(l, u0 + ustep * n + p)
                    act.wait_ge(unit_done, l * UNITS + (u0 + ustep * n + ustep))
                    act.activation(sq8[:, n, :], bank[n % 4][:, 0:T], ACT.Square).then_inc(sq_done, 1)

            def halves_of_h(l, sub):
                for k in range(KT):
                    act.wait_ge(h_value, l * 16 + (8 * sub + k + 1))
                    act.activation(hhi[:, k, :], acc[:, k, :], ACT.Copy).then_inc(h_hi, 1)

            act.wait_ge(x_loaded, 16)
            for k in range(KT):
                act.activation(sq8[:, k, :], x[:, k, :], ACT.Square).then_inc(sq_done, 1)
            act.wait_ge(memset_done, 3)
            log_table(0, 0)
            def half_of_z(l, k):
                act.wait_ge(conv_norm, l * 24 + (16 + k + 1))
                act.activation(zhi[:, k, :], acc[:, k, :], ACT.Copy).then_inc(z_hi, 1)

            for s in range(AHEAD):
                act.wait_ge(w_ready[s], 16)
                act.activation(whi[s][:, :, :], wring[s][:, :, :], ACT.Copy).then_inc(hi_done, 1)
            with act.Fori(0, DEPTH) as l:
                act.wait_ge(stat_done, l * STATS + 1)
                rsqrt(l, X[:, 0:T], 0, 0)
                halves_of_h(l, 0)
                for n in range(KT):
                    split(l, U_CIN + 2 * n)
                    if n >= 4:
                        act.wait_ge(u_ready, l * 16 + (2 * (n - 4) + 2))
                    gemm(l, U_CIN + 2 * n)
                    sigmoid(sig[:, n % 4, :], bank[(2 * n) % 4][:, 0:T])
                    split(l, U_CIN + 2 * n + 1)
                head(l, 0, True)
                with act.Fori(1, HEADS) as hd:
                    head(l, hd, False)
                act.wait_ge(aux_done, (l * HEADS + (HEADS - 1)) * AUX_HEAD + (A_S + 1))
                act.wait_ge(qd_ready, l * HEADS + HEADS)
                for n in range(KT):
                    split(l, U_GB + n)
                    late(l, HEADS - 1, n)
                    gemm(l, U_GB + n)
                    sigmoid(sgb[:, n, :], bank[n % 4][:, 0:T], bias=g_(G_GATE + 8 + n))
                    if n >= 5:
                        c = n - 5
                        act.wait_ge(ret_norm, l * (HEADS * 6) + 6 * (c + 1))
                        act.activation(ghi[:, 4 * c:4 * c + 4, :], go[:, 4 * c:4 * c + 4, :], ACT.Copy).then_inc(g_hi, 1)
                late(l, HEADS - 1, 8)
                act.wait_ge(pst_stored, l * (HEADS * 16) + HEADS * 16)
                for j in range(4):
                    act.wait_ge(ret_norm, l * (HEADS * 6) + ((HEADS - 1) * 6 + 5 + j // 2))
                    act.activation(ghi[:, 12 + j, :], go[:, 12 + j, :], ACT.Copy).then_inc(g_hi, 1)
                for n in range(KT):
                    split(l, U_RET + 3 * n)
                    if n < 4:
                        act.wait_ge(sg_ready, l * 16 + (12 + n + 1))
                    else:
                        act.wait_ge(ret_gated, l * 8 + (n - 3))
                    gemm(l, U_RET + 3 * n)
                    sigmoid(sig[:, n % 4, :], bank[(2 * n) % 4][:, 0:T], bias=g_(G_GATE + n))
                    split(l, U_RET + 3 * n + 1)
                    split(l, U_RET + 3 * n + 2)
                    if n == 2:
                        act.wait_ge(stat_done, l * STATS + (ST_CMEAN + 1))
                        act.activation(cmean[:, :], X[:, 0:T], ACT.Copy).then_inc(stat_read, 1)
                    if n == 3:
                        act.wait_ge(g_ready, l * 7 + 7)
                        for k in range(KT):
                            act.wait_ge(conv_norm, l * 24 + (k + 1))
                            act.activation(sqz[:, k, :], acc[:, k, :], ACT.Square).then_inc(sq_done, 1)
                    if n == 5:
                        log_table(l, RS_CONV)
                        act.wait_ge(stat_done, l * STATS + (ST_CVAR + 1))
                        rsqrt(l, X[:, 0:T], ST_CVAR, RS_CONV)
                    if n >= 6:
                        for k in range(4 * (n - 6), 4 * (n - 6) + 4):
                            act.wait_ge(conv_norm, l * 24 + (8 + k + 1))
                            if k >= 4:
                                act.wait_ge(conv_norm, l * 24 + (16 + k - 3))
                            act.activation(tmp[:, k % 4, :], acc[:, k, :], ACT.Sigmoid, bias=g_(G_LNB + k)).then_inc(zsig_done, 1)
                            if k:
                                half_of_z(l, k - 1)
                half_of_z(l, KT - 1)
                for n in range(KT):
                    split(l, U_CO + n)
                    act.wait_ge(merge_step, l * 16 + (2 * n + 2))
                    act.activation(hhi[:, n, :], acc2[:, n, :], ACT.Copy).then_inc(m_hi, 1)
                squares_of_products(l, U_WO, 1, SQ_POST)
                log_table(l, RS_POST)
                act.wait_ge(stat_done, l * STATS + (ST_POST + 1))
                rsqrt(l, X[:, 0:T], ST_POST, RS_POST)
                for k in range(KT):
                    act.wait_ge(post_step, l * POSTS + (k // 2 * 2 + 2))
                    act.activation(sq8[:, k, :], x[:, k, :], ACT.Square).then_inc(sq_done, 1)
                log_table(l, RS_FFN)
                act.wait_ge(stat_done, l * STATS + (ST_FFN + 1))
                rsqrt(l, X[:, 0:T], ST_FFN, RS_FFN)
                halves_of_h(l, 1)

                def f_half(n):
                    act.wait_ge(ffn_step, l * (2 * FT) + (2 * n + 2))
                    act.activation(fhi[:, n, :], tmp[:, n % 4, :], ACT.Copy).then_inc(f_hi, 1)

                for n in range(FT):
                    split(l, U_GU + 2 * n)
                    if n >= 4:
                        act.wait_ge(ffn_step, l * (2 * FT) + (2 * (n - 4) + 1))
                    gemm(l, U_GU + 2 * n)
                    sigmoid(sig[:, n % 4, :], bank[(2 * n) % 4][:, 0:T])
                    if n:
                        f_half(n - 1)
                    split(l, U_GU + 2 * n + 1)
                f_half(FT - 1)
                squares_of_products(l, U_DOWN, 3, SQ_POST2)
                log_table(l, RS_POST2)
                act.wait_ge(stat_done, l * STATS + (ST_POST2 + 1))
                rsqrt(l, X[:, 0:T], ST_POST2, RS_POST2)
                for k in range(KT):
                    act.wait_ge(post_step, l * POSTS + (8 + k // 2 * 2 + 2))
                    act.activation(sq8[:, k, :], x[:, k, :], ACT.Square).then_inc(sq_done, 1)
                log_table(l, RSTDS)

        @block.vector
        def _(dve):
            def lower(dst, value, hi):
                return dve.tensor_tensor(dst, value, hi.bitcast(F32), ALU.subtract)

            def split(l, u, hd=0):
                v = u + AHEAD
                s = v % RING
                if isinstance(hd, int):
                    dve.wait_ge(hi_done, l * UNITS + (v + 1 + hd * HEAD_UNITS))
                else:
                    dve.wait_ge(hi_done, l * UNITS + hd * HEAD_UNITS + (v + 1))
                lower(wlo[s][:, :, :], wring[s][:, :, :], whi[s][:, :, :]).then_inc(lo_done, 1)

            def normalised(l, sub, rs, gain):
                dve.wait_ge(rstd_done, l * RSTDS + (rs + 1))
                for k in range(KT + 2):
                    if k < KT:
                        dve.scalar_tensor_tensor(out=acc[:, k, :], in0=x[:, k, :], scalar=g_(gain + k), in1=rstd[:, :],
                                                 op0=ALU.mult, op1=ALU.mult).then_inc(h_value, 1)
                    if k >= 2:
                        dve.wait_ge(h_hi, l * 16 + (8 * sub + k - 1))
                        lower(hlo[:, k - 2, :], acc[:, k - 2, :], hhi[:, k - 2, :]).then_inc(h_ready, 1)

            def conv_tap(l, pair, k):
                for i in range(2):
                    n = pair * 2 + i
                    tap = par[:, ds(n * TAPS + (G_CW + k), 1)]
                    out = acc[:, ds(n, 1), 0:SEQ].rearrange("p o t -> p (o t)")
                    src = up[:, ds(n, 1), k:k + SEQ].rearrange("p o t -> p (o t)")
                    if k == 0:
                        dve.tensor_scalar(out, src, tap, par[:, ds(n + G_CB, 1)], ALU.mult, ALU.add).then_inc(conv_step, 1)
                    else:
                        dve.wait_ge(conv_step, l * (KT * CONVS) + pair * (2 * CONVS) + (2 * (k - 1) + i + 1))
                        dve.scalar_tensor_tensor(out=out, in0=src, scalar=tap, in1=out, op0=ALU.mult, op1=ALU.add).then_inc(conv_step, 1)

            def conv_taps(l, pair, a, b):
                for k in range(a, b):
                    conv_tap(l, pair, k)

            def rope(l, hd, i, first):
                H = l * HEADS + hd
                base = H * ROPES + 6 * i
                x1, x2 = bank[2 * i][:, 0:T], bank[2 * i + 1][:, 0:T]
                dve.wait_ge(unit_done, l * UNITS + hd * HEAD_UNITS + (U_HEAD + 2 * i + 2))
                if i == 1:
                    dve.wait_ge(rope_step, base)
                cos, sin = col(C_COS, T), col(C_SIN, T)
                for n, (a, b) in enumerate(((x1, cos), (x2, sin), (x1, sin), (x2, cos))):
                    dve.tensor_tensor(tmp[:, n, :], a, b, ALU.mult).then_inc(rope_step, 1)
                dve.wait_ge(rope_step, base + 2)
                dve.tensor_tensor(qkv[:, 2 * i, :], tmp[:, 0, :], tmp[:, 1, :], ALU.subtract).then_inc(rope_step, 1)
                dve.wait_ge(rope_step, base + 4)
                dve.tensor_tensor(qkv[:, 2 * i + 1, :], tmp[:, 2, :], tmp[:, 3, :], ALU.add).then_inc(rope_step, 1)

            def update(l, hd, b, d):
                pos = A_U + 2 * b + d
                dve.wait_ge(aux_done, (l * HEADS + hd) * AUX_HEAD + (pos + 1))
                st = state[b % RING][:, d, :]
                dve.scalar_tensor_tensor(out=st, in0=st, scalar=con[:, ds(hd + C_CD, 1)], in1=aux[pos % 3][:, :],
                                         op0=ALU.mult, op1=ALU.add).then_inc(dve_aux, 1)

            def centre(l, hd):
                H = l * HEADS + hd
                dve.wait_ge(aux_done, H * AUX_HEAD + (A_MEAN + 1))
                mean = aux[A_MEAN % 3][:, 0:T].rearrange("p (o t) -> p o t", o=1).to_broadcast([P, 4, T])
                dve.tensor_tensor(oT[:, :, :], oT[:, :, :], mean, ALU.subtract).then_inc(dve_aux, 1)

            def normalise(l, hd, last=False):
                H = l * HEADS + hd
                dve.wait_ge(rope_step, (H + (1 if last else 2)) * ROPES)
                dve.wait_ge(dve_aux, H * AUX_DVE + 20)
                dve.wait_ge(rstd_done, l * RSTDS + (hd + (RS_RET + 1)))
                for e in range(4):
                    dve.scalar_tensor_tensor(out=tmp[:, e, :], in0=oT[:, e, :], scalar=par[:, ds(hd * 4 + (G_RET + e), 1)],
                                             in1=rstd[:, :], op0=ALU.mult, op1=ALU.mult).then_inc(ret_norm, 1)
                dve.wait_ge(ret_norm, H * 6 + 4)
                dve.wait_ge(sg_ready, H * 4 + 4)
                for e in range(0, 4, 2):
                    dve.tensor_tensor(go[:, ds(hd * 4 + e, 2), :], tmp[:, e:e + 2, :], sg[:, e:e + 2, :], ALU.mult).then_inc(ret_norm, 1)

            def gate(l, hd, j, first):
                if j == 0 and not first:
                    dve.wait_ge(ret_norm, (l * HEADS + hd) * 6)
                dve.wait_ge(sig_done, l * SIGS + hd * 4 + (SIG_G + j + 1))
                dve.tensor_tensor(sg[:, j, :], bank[j][:, 0:T], sig[:, j, :], ALU.mult).then_inc(sg_ready, 1)

            def decayed_keys(l, hd):
                H = l * HEADS + hd
                dve.wait_ge(aux_done, H * AUX_HEAD + (A_KT + 1))
                dec = con[:, ds(hd * 2 + C_KDEC, 2)].rearrange("p (c o) -> p c o", o=1).to_broadcast([P, 2, DK])
                dve.tensor_tensor(kdec[:, :, :], aux[0][:, :].rearrange("p (c d) -> p c d", c=2), dec, ALU.mult).then_inc(dve_aux, 1)
                dve.wait_ge(kd_ready, H + 1)
                lower(khl[64:P, :], kd[64:P, :], khl[64:P, :]).then_inc(khl_step, 1)
                dve.wait_ge(khl_step, H + 1)
                own = con[:, C_OWN:C_OWN + DB].rearrange("p (b o) -> p b o", o=1).to_broadcast([P, DB, DK])
                src = khl[:, :].bitcast(F32).rearrange("p (o d) -> p o d", o=1).to_broadcast([P, DB, DK])
                dve.tensor_tensor(kdecs[:, :, :], src, own, ALU.mult).then_inc(ks_ready, 1)

            def values_low(l, hd):
                H = l * HEADS + hd
                dve.wait_ge(vs_hi, H * 2 + 2)
                lower(vslo[:, :], aux[(A_V + 2) % 3][:, :], vshi[:, :]).then_inc(dve_aux, 1)

            def decayed_queries(l, hd, first):
                dve.wait_ge(rope_step, (l * HEADS + hd) * ROPES + ROPES)
                if not first:
                    dve.wait_ge(stat_done, l * STATS + (hd + ST_X))
                dve.tensor_tensor(qd[:, :, :], qkv[:, 0:2, SEQ:T],
                                  con[:, ds(hd * 64 + C_QDEC, 64)].rearrange("p (o t) -> p o t", o=1).to_broadcast([P, 2, 64]),
                                  ALU.mult).then_inc(qd_ready, 1)

            def masked_scores(l, hd):
                dve.wait_ge(aux_done, (l * HEADS + hd) * AUX_HEAD + (A_S + 1))
                b = aux[A_S % 3]
                dve.tensor_tensor(stm[0:64, SEQ + P:MASKW], b[0:64, SEQ + P:MASKW], con[0:64, ds(hd * MASKW + (C_MASK + SEQ + P), 64)],
                                  ALU.mult).then_inc(sample_masked, 1)
                dve.tensor_tensor(stm[:, 0:SEQ + P], b[:, 0:SEQ + P], con[:, ds(hd * MASKW + C_MASK, SEQ + P)], ALU.mult).then_inc(dve_aux, 1)

            def head(l, hd, first):
                taps = (2, 1, 2, 1, 2, 1, 1, 1, 1, 0, 0, 1) if first else (4, 2, 4, 2, 4, 6, 2, 4, 2, 0, 0, 1)
                for j in range(HEAD_UNITS):
                    split(l, U_HEAD + j, hd)
                    t0 = 18 if first else 0
                    t = t0 + sum(taps[:j])
                    if not first and 1 <= j <= 4:
                        for i in range(4):
                            conv_taps(l, hd, t, t + (i < taps[j]))
                            t += i < taps[j]
                            update(l, hd - 1, 2 * (j - 1) + i // 2, i % 2)
                    conv_taps(l, hd, t, t0 + sum(taps[:j + 1]))
                    if j == 1 or j == 3:
                        rope(l, hd, j // 2, first)
                    if j == 5 and not first:
                        centre(l, hd - 1)
                    if j == 9:
                        decayed_keys(l, hd)
                        masked_scores(l, hd)
                        if not first:
                            normalise(l, hd - 1)
                        gate(l, hd, 0, first)
                    if j >= 9:
                        gate(l, hd, j - 8, first)
                        if j == 10:
                            decayed_queries(l, hd, first)
                values_low(l, hd)

            dve.memset(ones_d[:, :], 1.0 / D).then_inc(memset_done, 1)
            dve.memset(ones_v[:, :], 1.0 / DV).then_inc(memset_done, 1)
            dve.memset(eps[:, :], EPS).then_inc(memset_done, 1)
            for s in range(AHEAD):
                dve.wait_ge(hi_done, s + 1)
                lower(wlo[s][:, :, :], wring[s][:, :, :], whi[s][:, :, :]).then_inc(lo_done, 1)
            with dve.Fori(0, DEPTH) as l:
                dve.wait_ge(par_loaded, l * 16 + 16)
                normalised(l, 0, 0, G_MIXPRE)
                dve.memset(up[:, :, 0:PAD], 0.0).then_inc(pad_zeroed, 1)
                dve.wait_ge(u_loaded, l * 16 + 16)
                dve.wait_ge(pad_zeroed, l + 1)
                for n in range(KT):
                    split(l, U_CIN + 2 * n)
                    split(l, U_CIN + 2 * n + 1)
                    dve.wait_ge(unit_done, l * UNITS + (U_CIN + 2 * n + 2))
                    dve.wait_ge(sig_done, l * SIGS + (n + 1))
                    b, s = bank[(2 * n + 1) % 4], sig[:, n % 4, :]
                    dve.tensor_tensor(up[:, n, PAD:PAD + SEQ], b[:, 0:SEQ], s[:, 0:SEQ], ALU.mult).then_inc(u_ready, 1)
                    dve.tensor_tensor(us[:, n, :, PAD:PAD + DS], b[:, SEQ:T].rearrange("p (b t) -> p b t", b=DB),
                                      s[:, SEQ:T].rearrange("p (b t) -> p b t", b=DB), ALU.mult).then_inc(u_ready, 1)
                    if n >= 2:
                        dve.wait_ge(u_ready, l * 16 + 4)
                        conv_taps(l, 0, 3 * (n - 2), 3 * (n - 1))
                dve.wait_ge(u_ready, l * 16 + 16)
                dve.wait_ge(con_loaded, 16)
                head(l, 0, True)
                with dve.Fori(1, HEADS) as hd:
                    head(l, hd, False)
                last = HEADS - 1

                def gated_low(c):
                    dve.wait_ge(g_hi, l * 7 + (c + 1))
                    lower(glo[:, 4 * c:4 * c + 4, :], go[:, 4 * c:4 * c + 4, :], ghi[:, 4 * c:4 * c + 4, :]).then_inc(g_ready, 1)

                for n in range(KT):
                    split(l, U_GB + n)
                    if 1 <= n <= 4:
                        for i in range(4):
                            update(l, last, 2 * (n - 1) + i // 2, i % 2)
                    if n == 5:
                        centre(l, last)
                    if n == 6:
                        dve.wait_ge(pst_stored, l * (HEADS * 16) + HEADS * 16)
                        for s in range(RING):
                            dve.wait_ge(r_stored[s], l * (HEADS * 32) + HEADS * 32)
                        gated_low(0)
                    if n == 7:
                        gated_low(1)
                        gated_low(2)
                dve.wait_ge(sample_conv_step, l * (2 * TAPS) + 2 * TAPS)
                normalise(l, last, True)
                for j in range(4):
                    dve.wait_ge(g_hi, l * 7 + (3 + j + 1))
                    lower(glo[:, 12 + j, :], go[:, 12 + j, :], ghi[:, 12 + j, :]).then_inc(g_ready, 1)
                def z_low(k):
                    dve.wait_ge(z_hi, l * 8 + (k + 1))
                    lower(zlo[:, k, :], acc[:, k, :], zhi[:, k, :]).then_inc(z_ready, 1)

                dve.wait_ge(u_saved, l * 32 + 32)
                dve.wait_ge(conv_step, l * (KT * CONVS) + KT * CONVS)
                dve.wait_ge(sample_conv_step, l * (2 * TAPS) + 2 * TAPS)
                for n in range(KT):
                    for p in range(3):
                        split(l, U_RET + 3 * n + p)
                    dve.wait_ge(sig_done, l * SIGS + (SIG_GA + n + 1))
                    dve.wait_ge(unit_done, l * UNITS + (U_RET + 3 * n + 3))
                    dve.tensor_tensor(acc2[:, n, :], bank[(2 * n + 1) % 4][:, 0:T], sig[:, n % 4, :], ALU.mult).then_inc(ret_gated, 1)
                    if n == 2:
                        dve.wait_ge(stat_read, l * STATS + (ST_CMEAN + 1))
                        for k in range(KT):
                            dve.tensor_tensor(acc[:, k, :], acc[:, k, :], cmean[:, :], ALU.subtract).then_inc(conv_norm, 1)
                    if n >= 6:
                        for k in range(4 * (n - 6), 4 * (n - 6) + 4):
                            dve.wait_ge(zsig_done, l * 8 + (k + 1))
                            dve.wait_ge(conv_norm, l * 24 + (8 + k + 1))
                            dve.scalar_tensor_tensor(out=acc[:, k, :], in0=acc[:, k, :], scalar=g_(G_LNB + k), in1=tmp[:, k % 4, :],
                                                     op0=ALU.add, op1=ALU.mult).then_inc(conv_norm, 1)
                            if k >= 2:
                                z_low(k - 2)
                    if n == 5:
                        dve.wait_ge(conv_norm, l * 24 + 8)
                        dve.wait_ge(rstd_done, l * RSTDS + (RS_CONV + 1))
                        for k in range(KT):
                            dve.scalar_tensor_tensor(out=acc[:, k, :], in0=acc[:, k, :], scalar=g_(G_LNG + k), in1=rstd[:, :],
                                                     op0=ALU.mult, op1=ALU.mult).then_inc(conv_norm, 1)
                for k in range(KT - 2, KT):
                    z_low(k)

                def merged_low(n):
                    dve.wait_ge(m_hi, l * 8 + (n + 1))
                    lower(hlo[:, n, :], acc2[:, n, :], hhi[:, n, :]).then_inc(m_ready, 1)

                for n in range(KT):
                    split(l, U_CO + n)
                    dve.wait_ge(unit_done, l * UNITS + (U_CO + n + 1))
                    dve.wait_ge(sig_done, l * SIGS + (SIG_GB + n + 1))
                    dve.tensor_tensor(tmp[:, n % 4, :], bank[n % 4][:, 0:T], sgb[:, n, :], ALU.mult).then_inc(merge_step, 1)
                    dve.wait_ge(merge_step, l * 16 + (2 * n + 1))
                    dve.wait_ge(ret_gated, l * 8 + (n + 1))
                    dve.tensor_tensor(acc2[:, n, :], acc2[:, n, :], tmp[:, n % 4, :], ALU.add).then_inc(merge_step, 1)
                    if n:
                        merged_low(n - 1)
                merged_low(KT - 1)

                def post(sub, rs, sq0, gain, u0, ustep):
                    for n in range(KT):
                        for p in range(ustep):
                            split(l, u0 + ustep * n + p)
                        dve.wait_ge(sq_done, l * SQS + (sq0 + n + 1))
                        dve.tensor_scalar(acc[:, n, :], bank[n % 4][:, 0:T], g_(gain + n), None, ALU.mult).then_inc(y_copied, 1)
                    dve.wait_ge(rstd_done, l * RSTDS + (rs + 1))
                    dve.wait_ge(y_copied, l * 16 + (8 * sub + 8))
                    scale = rstd[:, :].rearrange("p (o t) -> p o t", o=1).to_broadcast([P, 2, T])
                    for n in range(0, KT, 2):
                        y = tmp[:, n % 4:n % 4 + 2, :]
                        dve.tensor_tensor(y, acc[:, n:n + 2, :], scale, ALU.mult).then_inc(post_step, 1)
                        dve.wait_ge(post_step, l * POSTS + (8 * sub + n + 1))
                        dve.tensor_tensor(x[:, n:n + 2, :], x[:, n:n + 2, :], y, ALU.add).then_inc(post_step, 1)

                post(0, RS_POST, SQ_POST, G_MIXPOST, U_WO, 1)
                dve.wait_ge(post_step, l * POSTS + 8)
                normalised(l, 1, RS_FFN, G_FFNPRE)

                def ffn_low(n):
                    dve.wait_ge(f_hi, l * FT + (n + 1))
                    lower(flo[:, n, :], tmp[:, n % 4, :], fhi[:, n, :]).then_inc(f_ready, 1)

                for n in range(FT):
                    split(l, U_GU + 2 * n)
                    b = (2 * n) % 4
                    dve.wait_ge(sig_done, l * SIGS + (SIG_GATE + n + 1))
                    if n >= 4:
                        dve.wait_ge(f_ready, l * FT + (n - 3))
                    dve.tensor_tensor(tmp[:, n % 4, :], bank[b][:, 0:T], sig[:, n % 4, :], ALU.mult).then_inc(ffn_step, 1)
                    if n:
                        ffn_low(n - 1)
                    split(l, U_GU + 2 * n + 1)
                    dve.wait_ge(ffn_step, l * (2 * FT) + (2 * n + 1))
                    dve.wait_ge(unit_done, l * UNITS + (U_GU + 2 * n + 2))
                    dve.tensor_tensor(tmp[:, n % 4, :], bank[b + 1][:, 0:T], tmp[:, n % 4, :], ALU.mult).then_inc(ffn_step, 1)
                ffn_low(FT - 1)
                post(1, RS_POST2, SQ_POST2, G_FFNPOST, U_DOWN, 3)
                dve.wait_ge(post_step, l * POSTS + 16)


def constants():
    c = np.zeros((P, NCONST), np.float32)
    half = DK // 2
    freqs = (np.float32(10000.0) ** (-np.arange(half, dtype=np.float32) / np.float32(half))).astype(np.float32)
    pos = np.concatenate([np.arange(SEQ), np.tile(PAST + np.arange(DS), DB)]).astype(np.float32)
    ang = (pos[None, :] * freqs[:, None]).astype(np.float32).astype(np.float64)
    c[:, C_COS:C_COS + T], c[:, C_SIN:C_SIN + T] = np.cos(ang), np.sin(ang)
    scale = DK ** -0.5
    p = np.arange(P)
    for h in range(HEADS):
        g = float(np.log1p(-np.exp2(-5.0 - h)))
        j, i = p[:, None], np.arange(SEQ)[None, :]
        m = np.where(i >= j, np.exp(g * np.maximum(i - j, 0)), 0.0) * scale
        o = C_MASK + h * MASKW
        c[:, o:o + SEQ], c[:, o + SEQ:o + SEQ + P] = m, m[:, :P]
        j, i = p[:64, None], p[None, :64]
        c[:64, o + SEQ + P:o + MASKW] = np.where((i // DS == j // DS) & (i >= j), np.exp(g * np.maximum(i - j, 0)), 0.0) * scale
        c[:, C_KDEC + 2 * h] = np.exp(g * (SEQ - 1 - p)) * scale
        c[:, C_KDEC + 2 * h + 1] = np.exp(g * (P - 1 - p)) * scale
        c[:, C_KROW + h] = np.exp(g * (DS - 1 - p % DS)) * scale
        c[:, C_QDEC + 64 * h:C_QDEC + 64 * (h + 1)] = np.exp(g * (p[:64] % DS + 1.0))
        c[:, C_CD + h] = math.exp(g * DS)
    c[:, C_OWN:C_OWN + DB] = p[:, None] % (DB * DS) // DS == np.arange(DB)
    c[:, C_ID:C_ID + P] = np.eye(P)
    return c


def units_of(w_in, w_ret_out, w_conv_out, w_o, w_gate, w_up, w_down):
    def tiles(w):
        k, n = w.shape
        t = w.reshape(k // P, P, n // P, P).transpose(2, 1, 0, 3)
        if k // P % UB:
            pad = np.zeros((n // P, P, -(k // P) % UB, P), w.dtype)
            t = np.concatenate([t, pad], axis=2)
        return t.reshape(n // P, P, -1, UB, P).transpose(0, 2, 1, 3, 4)

    win = tiles(w_in)
    q, k, v, g, ca, cb, ga, gb = (win[a // P:b // P] for a, b in zip(
        (0, 1024, 2048, 4096, 6144, 7168, 8192, 9216), (1024, 2048, 4096, 6144, 7168, 8192, 9216, 10240)))
    out = []
    for n in range(KT):
        out += [cb[n], ca[n]]
    for h in range(HEADS):
        out += [*q[2 * h:2 * h + 2], *k[2 * h:2 * h + 2], *v[4 * h:4 * h + 4], *g[4 * h:4 * h + 4]]
    out += list(gb)
    ret = tiles(w_ret_out)
    for n in range(KT):
        out += [ga[n], ret[n]]
    out += [*tiles(w_conv_out), *tiles(w_o)]
    gate, upw = tiles(w_gate), tiles(w_up)
    for n in range(FT):
        out += [gate[n], upw[n]]
    out += list(tiles(w_down))
    return np.concatenate(out)


def kernel(x_prompt, x_sample, state_ret, state_conv, g_mix_pre, g_mix_post, g_ffn_pre, g_ffn_post, w_in, b_gate,
           ret_gn_gain, w_ret_out, conv_w, conv_b, conv_ln_g, conv_ln_b, w_conv_out, w_o, w_ffn_gate, w_ffn_up, w_ffn_down):
    import concourse.bacc as bacc
    from concourse.bass_utils import run_bass_kernel_spmd

    a = {k: np.asarray(v) for k, v in locals().items() if k not in ("bacc", "run_bass_kernel_spmd")}
    feat = lambda v: v.reshape(DEPTH, -1, P).transpose(2, 0, 1)
    x = np.concatenate([a["x_prompt"][0], a["x_sample"].reshape(DB * DS, D)])
    params = np.concatenate(
        [feat(a[k]) for k in ("g_mix_pre", "g_mix_post", "g_ffn_pre", "g_ffn_post", "b_gate", "ret_gn_gain", "conv_b", "conv_ln_g", "conv_ln_b")]
        + [a["conv_w"].reshape(DEPTH, TAPS, KT, P).transpose(3, 0, 2, 1).reshape(P, DEPTH, -1)], axis=2)
    c_in = np.zeros((DEPTH, P, KT, DB, DS + PAD), np.float32)
    c_in[..., 0:PAD] = a["state_conv"].reshape(DEPTH, DB, PAD, KT, P).transpose(0, 4, 3, 1, 2)
    arrays = {
        "w": np.concatenate([units_of(*(a[k][l] for k in ("w_in", "w_ret_out", "w_conv_out", "w_o", "w_ffn_gate", "w_ffn_up", "w_ffn_down")))
                             for l in range(DEPTH)] + [np.zeros((RING, P, UB, P), np.float32)]),
        "xin": x.T.reshape(KT, P, T).transpose(1, 0, 2),
        "consts": constants(),
        "params": np.concatenate([params.transpose(1, 0, 2), np.zeros((1, P, NPAR), np.float32)]),
        "r_in": a["state_ret"].transpose(0, 2, 1, 3, 4).reshape(DEPTH * HEADS * DB, 2, P, DV).transpose(0, 2, 1, 3),
        "c_in": c_in,
    }
    arrays = {k: np.ascontiguousarray(v) for k, v in arrays.items()}
    outs = {
        "x_out": (P, KT, T), "rp_out": (DEPTH * HEADS, P, 2, DV), "rs_out": (DEPTH * HEADS * DB, P, 2, DV),
        "cp_out": (DEPTH, P, KT, SEQ + PAD), "cs_out": (DEPTH, P, KT, DB, DS + PAD),
    }
    nc = bacc.Bacc("TRN2", target_bir_lowering=False, num_devices=1, dynamic_dma_scratch_size=4096)
    args = [nc.dram_tensor(k, v.shape, F32, kind="ExternalInput").ap() for k, v in arrays.items()]
    args += [nc.dram_tensor(k, s, F32, kind="ExternalOutput").ap() for k, s in outs.items()]
    program(nc, *args)
    r = run_bass_kernel_spmd(nc, [arrays], core_ids=[0]).results[0]
    y = r["x_out"].transpose(1, 0, 2).reshape(D, T).T
    rp = r["rp_out"].reshape(DEPTH, 1, HEADS, P, 2, DV).transpose(0, 1, 2, 4, 3, 5).reshape(DEPTH, 1, HEADS, DK, DV)
    rs = r["rs_out"].reshape(DEPTH, HEADS, DB, P, 2, DV).transpose(0, 2, 1, 4, 3, 5).reshape(DEPTH, DB, HEADS, DK, DV)
    cp = r["cp_out"][..., SEQ:].transpose(0, 3, 2, 1).reshape(DEPTH, 1, PAD, D)
    cs = r["cs_out"][..., DS:].transpose(0, 3, 4, 2, 1).reshape(DEPTH, DB, PAD, D)
    return tuple(np.ascontiguousarray(v) for v in (y[:SEQ].reshape(1, SEQ, D), y[SEQ:].reshape(DB, DS, D), rp, cp, rs, cs))
```

```python
import math
from contextlib import ExitStack

import numpy as np

import concourse.bass as bass
from concourse import mybir

F32 = mybir.dt.float32
F32R = mybir.dt.float32r
ALU = mybir.AluOpType
ACT = mybir.ActivationFunctionType
ds = bass.ds

P = 128
D = 1024
DEPTH = 2
SEQ = 256
DB, DS = 8, 8
PAST = 2048
T = SEQ + DB * DS
HEADS = 4
DK, DV = 256, 512
TAPS = 31
PAD = TAPS - 1
FF = 2816
EPS = 1e-6
KT = D // P
FT = FF // P
VT = HEADS * DV // P
UB = 8
RING = 4
SBUF_END = 229344
AHEAD = 3

U_CIN, U_HEAD, U_GB, U_RET, U_CO, U_WO, U_GU, U_DOWN, UNITS = 0, 16, 64, 72, 96, 104, 112, 156, 180
HEAD_UNITS = 12
SIGS, SIG_G, SIG_GB, SIG_GA, SIG_GATE = 62, 8, 24, 32, 40
SQS, SQ_RET, SQ_CONV, SQ_POST, SQ_FFN, SQ_POST2 = 44, 8, 12, 20, 28, 36
STATS, ST_X, ST_CMEAN, ST_CVAR, ST_POST, ST_FFN, ST_POST2 = 10, 1, 5, 6, 7, 8, 9
RSTDS, RS_RET, RS_CONV, RS_POST, RS_FFN, RS_POST2 = 9, 1, 5, 6, 7, 8
AUX_HEAD, AUX_ACT, AUX_DVE = 28, 8, 20
ROPES, CONVS, POSTS = 12, TAPS, 16
LATE_TAPS = 5

A_KT, A_KTS, A_S, A_V, A_P, A_U, A_PU, A_MEAN, A_VAR = 0, 1, 2, 3, 6, 8, 24, 26, 27
READER = ([("dve", 0), ("act", 0), ("dve", 1), ("act", 1), ("act", 2), ("dve", 2), ("act", 3), ("act", 4)]
          + [("dve", 3 + i) for i in range(16)] + [("act", 5), ("act", 6), ("dve", 19), ("act", 7)])
BEFORE = {0: 27, 1: 25, 2: 26}

C_COS, C_SIN, C_MASK, C_KDEC, C_KROW, C_OWN, C_QDEC, C_CD, C_ID = 0, 320, 640, 2432, 2440, 2444, 2452, 2708, 2712
NCONST = C_ID + P
MASKW = 448
G_MIXPRE, G_MIXPOST, G_FFNPRE, G_FFNPOST, G_GATE, G_RET, G_CB, G_LNG, G_LNB, G_CW = 0, 8, 16, 24, 32, 48, 64, 72, 80, 88
NPAR = G_CW + KT * TAPS


def program(nc, w, xin, consts, params, r_in, c_in, x_out, rp_out, rs_out, cp_out, cs_out):
    ctx = ExitStack()
    with ctx:
        def sem(name):
            return ctx.enter_context(nc.semaphore(name))

        at = [-(-nc.sbuf_base // 32) * 32]

        def sb(name, *shape, dtype=F32, offset=None):
            where = at[0] if offset is None else offset
            if offset is None:
                at[0] += -(-4 * math.prod(shape) // 32) * 32
            return nc.alloc_sbuf_tensor_at(name, [P, *shape], dtype, offset=where)

        wring = [sb(f"wring{i}", UB, P) for i in range(RING)]
        whi = [sb(f"whi{i}", UB, P, dtype=F32R) for i in range(RING)]
        wlo = [sb(f"wlo{i}", UB, P, dtype=F32R) for i in range(RING)]
        x = sb("x", KT, T)
        hhi, hlo = sb("hhi", KT, T, dtype=F32R), sb("hlo", KT, T, dtype=F32R)
        acc = sb("acc", KT, T)
        rstd = sb("rstd", T)
        lnv = sb("lnv", T)
        cmean = lnv
        sig = sb("sig", 4, T)
        tmp = sb("tmp", 4, T)
        con = sb("con", NCONST)
        par = sb("par", NPAR)
        ones_d = sb("ones_d", P)
        ones_v = sb("ones_v", P)
        eps = sb("eps", 1)
        qkv_at = at[0]
        qkv = sb("qkv", 8, T)
        sgb = sb("sgb", KT, T, offset=qkv_at)
        sq8 = sb("sq8", KT, T, offset=qkv_at)
        go_at = at[0]
        go = sb("go", VT, T)
        zhi = sb("zhi", KT, T, dtype=F32R, offset=go_at)
        zlo = sb("zlo", KT, T, dtype=F32R, offset=go_at + KT * T * 4)
        sqz = sb("sqz", KT, T, offset=go_at + KT * T * 4)
        up_at = at[0]
        up = sb("up", KT, SEQ + PAD)
        us = sb("us", KT, DB, DS + PAD)
        stap = sb("stap", KT, DB, DS, offset=go_at + (HEADS - 1) * 4 * T * 4)
        acc2 = sb("acc2", KT, T, offset=up_at)
        csum = sb("csum", 4, T, offset=up_at + 4 * KT * T)
        head_at = at[0]
        kdec = sb("kdec", 2, DK)
        kdecs = sb("kdecs", DB, DK, dtype=F32R)
        vtok = sb("vtok", 3, DV)
        vshi, vslo = sb("vshi", DV, dtype=F32R), sb("vslo", DV, dtype=F32R)
        stm = sb("stm", MASKW)
        qd = sb("qd", 2, DB * DS)
        pst = sb("pst", 2, DV)
        state = [sb(f"state{i}", 2, DV) for i in range(RING)]
        sg = sb("sg", 4, T)
        oT = sb("oT", 4, T)
        sqo_at = at[0]
        sqo = sb("sqo", 4, T)
        kdup = sb("kdup", 2, P, offset=sqo_at)
        vdup = sb("vdup", 4, P, offset=sqo_at + 8 * P)
        kd = sb("kd", DK, offset=sqo_at + 24 * P)
        khl = sb("khl", DK, dtype=F32R, offset=sqo_at + 32 * P)
        ghi = sb("ghi", VT, T, dtype=F32R, offset=head_at)
        glo = sb("glo", VT, T, dtype=F32R, offset=head_at + VT * T * 4)
        fhi = sb("fhi", FT, T, dtype=F32R, offset=go_at)
        flo = sb("flo", FT, T, dtype=F32R, offset=go_at + FT * T * 4)
        assert at[0] <= SBUF_END, at[0] - SBUF_END
        assert head_at + 2 * VT * T * 4 <= at[0] and go_at + 2 * FT * T * 4 <= at[0]

        bank = [ctx.enter_context(nc.psum_tensor(f"bank{i}", [P, 512], F32)) for i in range(8)]
        aux = bank[4:7]
        X = bank[7]

        w_ready = [sem(f"w_ready{i}") for i in range(RING)]
        hi_done, lo_done, unit_done = sem("hi_done"), sem("lo_done"), sem("unit_done")
        aux_done, act_aux, dve_aux = sem("aux_done"), sem("act_aux"), sem("dve_aux")
        sq_done, head_sum, conv_sum = sem("sq_done"), sem("head_sum"), sem("conv_sum")
        stat_done, stat_read, rstd_done, log_loaded = sem("stat_done"), sem("stat_read"), sem("rstd_done"), sem("log_loaded")
        sig_done, zsig_done = sem("sig_done"), sem("zsig_done")
        h_value, h_hi, h_ready = sem("h_value"), sem("h_hi"), sem("h_ready")
        g_hi, g_ready = sem("g_hi"), sem("g_ready")
        z_hi, z_ready = sem("z_hi"), sem("z_ready")
        m_hi, m_ready = sem("m_hi"), sem("m_ready")
        f_hi, f_ready = sem("f_hi"), sem("f_ready")
        rope_step, v_copied, qd_ready = sem("rope_step"), sem("v_copied"), sem("qd_ready")
        sample_masked, sg_ready, ret_norm = sem("sample_masked"), sem("sg_ready"), sem("ret_norm")
        dup_ready, kd_ready, khl_step, ks_ready = sem("dup_ready"), sem("kd_ready"), sem("khl_step"), sem("ks_ready")
        vs_hi = sem("vs_hi")
        pad_zeroed, u_ready = sem("pad_zeroed"), sem("u_ready")
        conv_step, sample_conv_step, conv_norm = sem("conv_step"), sem("sample_conv_step"), sem("conv_norm")
        ret_gated, merge_step = sem("ret_gated"), sem("merge_step")
        y_copied, post_step, ffn_step = sem("y_copied"), sem("post_step"), sem("ffn_step")
        memset_done = sem("memset_done")
        x_loaded, par_loaded, con_loaded = sem("x_loaded"), sem("par_loaded"), sem("con_loaded")
        u_loaded, u_saved = sem("u_loaded"), sem("u_saved")
        r_loaded = [sem(f"r_loaded{i}") for i in range(RING)]
        r_stored = [sem(f"r_stored{i}") for i in range(RING)]
        pst_stored, x_stored = sem("pst_stored"), sem("x_stored")

        def col(c0, n):
            return con[:, c0:c0 + n]

        def g_(c):
            return par[:, c:c + 1]

        block = ctx.enter_context(nc.Block())

        @block.sync
        def _(sp):
            sp.dma_start(x[:, :, :], xin).then_inc(x_loaded, 16)
            for s in range(RING):
                sp.dma_start(wring[s][:, :, :], w[s]).then_inc(w_ready[s], 16)
            with sp.Fori(1, DEPTH * UNITS // RING + 1) as i:
                for s in range(RING):
                    sp.wait_ge(lo_done, i * RING + (s + 1 - RING))
                    sp.dma_start(wring[s][:, :, :], w[i * RING + s]).then_inc(w_ready[s], 16)
            for s in range(RING):
                sp.wait_ge(w_ready[s], (DEPTH * UNITS // RING + 1) * 16)

        @block.gpsimd
        def _(pool):
            def load(l, j, s):
                pool.dma_start(state[s][:, :, :], r_in[l * (HEADS * DB) + j]).then_inc(r_loaded[s], 16)

            def sample_conv_tap(l, k, first=False):
                out = acc[:, :, SEQ:T].rearrange("p n (b t) -> p n b t", b=DB)
                weights = par[:, G_CW:G_CW + KT * TAPS].rearrange("p (n k) -> p n k", n=KT)
                tap = weights[:, :, ds(k, 1)].rearrange("p n (b t) -> p n b t", b=1).to_broadcast([P, KT, DB, DS])
                bias = par[:, G_CB:G_CB + KT].rearrange("p (n b t) -> p n b t", b=1, t=1).to_broadcast([P, KT, DB, DS])
                if not first:
                    pool.wait_ge(sample_conv_step, l * (2 * TAPS) + 2 * k)
                pool.tensor_tensor(out if first else stap[:, :, :, :], us[:, :, :, ds(k, DS)], tap, ALU.mult).then_inc(sample_conv_step, 1)
                pool.wait_ge(sample_conv_step, l * (2 * TAPS) + 2 * k + 1)
                pool.tensor_tensor(out, out, bias if first else stap[:, :, :, :], ALU.add).then_inc(sample_conv_step, 1)

            def head(l, hd, last):
                for b in range(DB):
                    pool.wait_ge(dve_aux, (l * HEADS + hd) * AUX_DVE + (3 + 2 * b + 2))
                    s = b % RING
                    pool.dma_start(rs_out[(l * HEADS + hd) * DB + b], state[s][:, :, :]).then_inc(r_stored[s], 16)
                    if b == DB - 1:
                        pool.wait_ge(act_aux, (l * HEADS + hd) * AUX_ACT + 5)
                        pool.wait_ge(stat_read, l * STATS + (hd + (ST_X + 1)))
                        pool.tensor_tensor(sqo[:, 0:2, :], oT[:, 0:2, :], oT[:, 2:4, :], ALU.add).then_inc(head_sum, 1)
                        pool.wait_ge(head_sum, (l * HEADS + hd) * 4 + 1)
                        pool.tensor_tensor(sqo[:, 0, :], sqo[:, 0, :], sqo[:, 1, :], ALU.add).then_inc(head_sum, 1)
                    if b and not (last and b > RING):
                        pool.wait_ge(r_stored[(b - 1) % RING], (l * HEADS + hd) * 32 + 16 * ((b - 1) // RING + 1))
                        load(l, hd * DB + (b - 1 + RING), (b - 1) % RING)
                if not last:
                    pool.wait_ge(r_stored[RING - 1], (l * HEADS + hd) * 32 + 32)
                    load(l, hd * DB + (DB - 1 + RING), RING - 1)
                pool.wait_ge(act_aux, (l * HEADS + hd) * AUX_ACT + 7)
                pool.dma_start(rp_out[l * HEADS + hd], pst[:, :, :]).then_inc(pst_stored, 16)
                pool.wait_ge(sq_done, l * SQS + (hd + (SQ_RET + 1)))
                pool.tensor_tensor(sqo[:, 0:2, :], sqo[:, 0:2, :], sqo[:, 2:4, :], ALU.add).then_inc(head_sum, 1)
                pool.wait_ge(head_sum, (l * HEADS + hd) * 4 + 3)
                pool.tensor_tensor(sqo[:, 0, :], sqo[:, 0, :], sqo[:, 1, :], ALU.add).then_inc(head_sum, 1)
                if not last:
                    for i in range(LATE_TAPS):
                        sample_conv_tap(l, hd * LATE_TAPS + (TAPS - (HEADS - 1) * LATE_TAPS + i))

            def sum_of_tiles(l, out, src, step):
                pool.tensor_tensor(out[:, 0:4, :], src[:, 0:4, :], src[:, 4:8, :], ALU.add).then_inc(conv_sum, 1)
                pool.wait_ge(conv_sum, l * 6 + (step + 1))
                pool.tensor_tensor(out[:, 0:2, :], out[:, 0:2, :], out[:, 2:4, :], ALU.add).then_inc(conv_sum, 1)
                pool.wait_ge(conv_sum, l * 6 + (step + 2))
                pool.tensor_tensor(out[:, 0, :], out[:, 0, :], out[:, 1, :], ALU.add).then_inc(conv_sum, 1)

            pool.dma_start(par[:, :], params[0]).then_inc(par_loaded, 16)
            pool.wait_ge(w_ready[1], 16)
            pool.dma_start(con[:, :], consts).then_inc(con_loaded, 16)
            with pool.Fori(0, DEPTH) as l:
                pool.dma_start(us[:, :, :, :], c_in[l]).then_inc(u_loaded, 16)
                for s in range(RING):
                    load(l, s, s)
                pool.wait_ge(u_ready, l * 16 + 16)
                pool.dma_start(cp_out[l], up[:, :, :]).then_inc(u_saved, 16)
                pool.dma_start(cs_out[l], us[:, :, :, :]).then_inc(u_saved, 16)
                for k in range(TAPS - (HEADS - 1) * LATE_TAPS):
                    sample_conv_tap(l, k, k == 0)
                with pool.Fori(0, HEADS - 1) as hd:
                    head(l, hd, False)
                pool.wait_ge(conv_step, l * (KT * CONVS) + KT * CONVS)
                pool.wait_ge(sample_conv_step, l * (2 * TAPS) + 2 * TAPS)
                pool.wait_ge(u_saved, l * 32 + 32)
                sum_of_tiles(l, csum, acc, 0)
                head(l, HEADS - 1, True)
                pool.wait_ge(sq_done, l * SQS + (SQ_CONV + KT))
                sum_of_tiles(l, sqz, sqz, 3)
                pool.wait_ge(u_saved, l * 32 + 32)
                pool.wait_ge(sample_conv_step, l * (2 * TAPS) + 2 * TAPS)
                for s in range(RING):
                    pool.wait_ge(r_stored[s], l * (HEADS * 32) + HEADS * 32)
                pool.wait_ge(unit_done, l * UNITS + UNITS)
                pool.wait_ge(y_copied, l * 16 + 16)
                pool.dma_start(par[:, :], params[l + 1]).then_inc(par_loaded, 16)
            for n in range(0, KT, 2):
                pool.wait_ge(post_step, (DEPTH - 1) * POSTS + (8 + n + 2))
                pool.dma_start(x_out[:, n:n + 2, :], x[:, n:n + 2, :]).then_inc(x_stored, 16)
            pool.wait_ge(x_stored, KT // 2 * 16)
            pool.wait_ge(par_loaded, (DEPTH + 1) * 16)
            pool.wait_ge(pst_stored, DEPTH * HEADS * 16)

        @block.tensor
        def _(pe):
            def unit(l, q, j, g, rhs, k0=0, n=UB, start=True, stop=True, ready=None, between=None):
                pe.wait_ge(lo_done, l * UNITS + q * RING + (j + 1))
                for k in range(n):
                    if ready is not None:
                        ready(k0 + k)
                    hi, lo = rhs(k0 + k)
                    pe.matmul(bank[g][:, 0:T], whi[j][:, k, :], hi, start=start and k == 0, stop=False)
                    pe.matmul(bank[g][:, 0:T], whi[j][:, k, :], lo, start=False, stop=False)
                    mm = pe.matmul(bank[g][:, 0:T], wlo[j][:, k, :], hi, start=False, stop=stop and k == n - 1)
                    if k == n - 1:
                        mm.then_inc(unit_done, 1)
                    if between is not None:
                        between(k)

            def tile_of(hi, lo):
                return lambda k: (hi[:, k, :], lo[:, k, :])

            h_tile = tile_of(hhi, hlo)

            def first_units(l, q, ready):
                pe.wait_ge(lo_done, l * UNITS + (q * RING + AHEAD))
                for k in range(UB):
                    ready(k)
                    for j in range(AHEAD):
                        pe.matmul(bank[j][:, 0:T], whi[j][:, k, :], hhi[:, k, :], start=(k == 0), stop=False)
                        pe.matmul(bank[j][:, 0:T], whi[j][:, k, :], hlo[:, k, :], start=False, stop=False)
                        mm = pe.matmul(bank[j][:, 0:T], wlo[j][:, k, :], hhi[:, k, :], start=False, stop=(k == UB - 1))
                        if k == UB - 1:
                            mm.then_inc(unit_done, 1)

            def keep_clock(n):
                for i in range(n):
                    pe.matmul(aux[0][:, 0:P], ones_d[:, :], ones_d[:, :], start=True, stop=True)

            def square_mean(l, sq0, k):
                pe.wait_ge(sq_done, l * SQS + (sq0 + k + 1))
                return pe.matmul(X[:, 0:T], ones_d[:, :], sq8[:, k, :], start=(k == 0), stop=(k == KT - 1))

            def aux_free(H, pos, first=False):
                if pos >= 3:
                    who, n = READER[pos - 3]
                elif first:
                    return
                else:
                    who, n = READER[BEFORE[pos]]
                    H = H - 1
                if who == "act":
                    pe.wait_ge(act_aux, H * AUX_ACT + (n + 1))
                else:
                    pe.wait_ge(dve_aux, H * AUX_DVE + (n + 1))

            def early(l, hd, j, first=False):
                H = l * HEADS + hd
                ident = con[:, C_ID:C_ID + P]

                def value_rows(c):
                    for e in range(4):
                        src = qkv[:, 4 + e, c * P:(c + 1) * P] if c < 2 else vdup[:, e, :]
                        mm = pe.transpose(aux[(A_V + c) % 3][:, e * P:(e + 1) * P], src, ident)
                    mm.then_inc(aux_done, 1)

                if j == 8:
                    aux_free(H, A_KT, first)
                    aux_free(H, A_KTS, first)
                    pe.wait_ge(rope_step, H * ROPES + ROPES)
                    for c in range(2):
                        for d in range(2):
                            mm = pe.transpose(aux[0][:, c * DK + d * P:c * DK + (d + 1) * P], qkv[:, 2 + d, c * P:(c + 1) * P], ident)
                    mm.then_inc(aux_done, 1)
                    pe.wait_ge(dup_ready, H * 2 + 1)
                    for d in range(2):
                        mm = pe.transpose(aux[1][:, d * P:(d + 1) * P], kdup[:, d, :], ident)
                    mm.then_inc(aux_done, 1)
                if j == 9:
                    aux_free(H, A_S, first)
                    b = aux[A_S % 3]
                    for o, j0, n, i0, m in ((0, 0, P, 0, SEQ), (SEQ, P, P, P, P), (SEQ + P, SEQ, 64, SEQ, 64)):
                        for d in range(2):
                            mm = pe.matmul(b[0:n, o:o + m], qkv[:, 2 + d, j0:j0 + n], qkv[:, d, i0:i0 + m],
                                           start=(d == 0), stop=(d == 1))
                    mm.then_inc(aux_done, 1)
                if j == 10:
                    pe.wait_ge(v_copied, H * 4 + 4)
                    for c in range(2):
                        aux_free(H, A_V + c)
                        value_rows(c)
                if j == 11:
                    pe.wait_ge(dup_ready, H * 2 + 2)
                    value_rows(2)

            def late_out(l, hd, p):
                H = l * HEADS + hd
                if p == 0:
                    pe.wait_ge(dve_aux, H * AUX_DVE + 2)
                    pe.wait_ge(act_aux, H * AUX_ACT + 3)
                aux_free(H, A_P + p)
                for i in range(2):
                    e = 2 * p + i
                    o = aux[(A_P + p) % 3]
                    pe.matmul(o[:, i * SEQ:(i + 1) * SEQ], vtok[:, 0, e * P:(e + 1) * P], stm[:, 0:SEQ], start=True, stop=False)
                    mm = pe.matmul(o[:, i * SEQ + P:(i + 1) * SEQ], vtok[:, 1, e * P:(e + 1) * P], stm[:, SEQ:SEQ + P],
                                   start=False, stop=True)
                mm.then_inc(aux_done, 1)

            def late_within(l, hd):
                pe.wait_ge(qd_ready, l * HEADS + hd + 1)
                pe.wait_ge(vs_hi, (l * HEADS + hd) * 2 + 1)
                for e in range(4):
                    pe.matmul(X[:, e * 64:(e + 1) * 64], vtok[0:64, 2, e * P:(e + 1) * P], stm[0:64, SEQ + P:MASKW],
                              start=(e == 0), stop=False, skip_group_check=True)

            def late_state(l, hd, b, d, half):
                H = l * HEADS + hd
                s = b % RING
                if b == 0 and d == 0 and half == 0:
                    pe.wait_ge(ks_ready, H + 1)
                    pe.wait_ge(dve_aux, H * AUX_DVE + 3)
                if d == 0 and half == 0:
                    pe.wait_ge(r_loaded[s], H * 32 + (b // RING + 1) * 16)
                for e in (2 * half, 2 * half + 1):
                    mm = pe.matmul(X[:, e * 64 + b * DS:e * 64 + (b + 1) * DS], state[s][:, d, e * P:(e + 1) * P],
                                   qd[:, d, b * DS:(b + 1) * DS], start=False, stop=(d == 1), skip_group_check=True)
                if b == DB - 1 and d == 1 and half == 1:
                    mm.then_inc(stat_done, 1)
                if half == 1:
                    pos = A_U + 2 * b + d
                    aux_free(H, pos)
                    pe.matmul(aux[pos % 3][:, :], kdecs[:, b, d * P:(d + 1) * P], vshi[:, :], start=True, stop=False)
                    pe.matmul(aux[pos % 3][:, :], kdecs[:, b, d * P:(d + 1) * P], vslo[:, :],
                              start=False, stop=True).then_inc(aux_done, 1)

            def late_prompt_state(l, hd, d):
                H = l * HEADS + hd
                pos = A_PU + d
                aux_free(H, pos)
                for c in range(2):
                    mm = pe.matmul(aux[pos % 3][:, :], kdec[:, c, d * P:(d + 1) * P], vtok[:, c, :],
                                   start=(c == 0), stop=(c == 1))
                mm.then_inc(aux_done, 1)

            def late_mean(l, hd):
                H = l * HEADS + hd
                aux_free(H, A_MEAN)
                pe.wait_ge(act_aux, H * AUX_ACT + 5)
                pe.wait_ge(stat_read, l * STATS + (hd + (ST_X + 1)))
                pe.wait_ge(head_sum, H * 4 + 2)
                pe.matmul(aux[A_MEAN % 3][:, 0:T], ones_v[:, :], sqo[:, 0, :], start=True, stop=True).then_inc(aux_done, 1)

            def late_var(l, hd):
                H = l * HEADS + hd
                aux_free(H, A_VAR)
                pe.wait_ge(head_sum, H * 4 + 4)
                pe.matmul(aux[A_VAR % 3][:, 0:T], ones_v[:, :], sqo[:, 0, :], start=True, stop=True).then_inc(aux_done, 1)

            def late(l, hd, j, k):
                if j == 0 and k in (4, 6):
                    late_out(l, hd, (k - 4) // 2)
                if j == 0 and k == 7:
                    late_within(l, hd)
                if 1 <= j <= 4:
                    late_state(l, hd, 2 * (j - 1) + k // 4, k % 4 // 2, k % 2)
                if j == 5 and k in (2, 5):
                    late_prompt_state(l, hd, k // 3)
                if j == 5 and k == 7:
                    late_mean(l, hd)
                if j == 7 and k == 7:
                    late_var(l, hd)

            def head(l, hd, first):
                H = l * HEADS + hd
                for j in range(HEAD_UNITS):
                    if j < 4 and first:
                        if j % 2 == 0:
                            pe.wait_ge(sig_done, l * SIGS + (7 + j // 2))
                        else:
                            pe.wait_ge(u_ready, l * 16 + (14 + j - 1))
                    elif j < 4:
                        pe.wait_ge(sg_ready, H * 4 + (j + 1 - 4))
                    elif j < 8:
                        pe.wait_ge(rope_step, H * ROPES + (3, 4, 9, 10)[j - 4])
                    else:
                        pe.wait_ge(v_copied, H * 4 + (j - 7))
                    if j == 11:
                        aux_free(H, A_V + 2)
                    unit(l, hd * 3 + (U_HEAD // RING + j // RING), j % RING, j % 4, h_tile,
                         between=None if first else lambda k: late(l, hd - 1, j, k))
                    early(l, hd, j, first)

            def h_read(l, k):
                pe.wait_ge(h_ready, l * 16 + (k + 1))

            pe.wait_ge(memset_done, 3)
            with pe.Fori(0, DEPTH) as l:
                for k in range(KT):
                    mean = square_mean(l, 0, k)
                mean.then_inc(stat_done, 1)
                keep_clock(20)
                first_units(l, 0, lambda k: h_read(l, k))
                unit(l, 0, AHEAD, AHEAD, h_tile)
                with pe.Fori(1, 4) as i:
                    for j in range(4):
                        if j % 2 == 0:
                            pe.wait_ge(sig_done, l * SIGS + i * 2 + (j // 2 - 1))
                        else:
                            pe.wait_ge(u_ready, l * 16 + i * 4 + (j - 3))
                        unit(l, i, j, j, h_tile)
                pe.wait_ge(con_loaded, 16)
                head(l, 0, True)
                with pe.Fori(1, HEADS) as hd:
                    head(l, hd, False)
                for n in range(KT):
                    if n < 4:
                        pe.wait_ge(sg_ready, l * 16 + (13 + n))
                    else:
                        pe.wait_ge(sig_done, l * SIGS + (SIG_GB + n - 3))
                    u = U_GB + n
                    unit(l, u // RING, u % RING, n % 4, h_tile, between=lambda k: late(l, HEADS - 1, n, k))
                for n in range(KT):
                    g = (2 * n) % 4
                    if n < 2:
                        pe.wait_ge(sig_done, l * SIGS + (SIG_GB + 5 + 2 * n))
                    else:
                        pe.wait_ge(sig_done, l * SIGS + (SIG_GA + n - 1))
                    u = U_RET + 3 * n
                    unit(l, u // RING, u % RING, g, h_tile)
                    if n < 2:
                        pe.wait_ge(sig_done, l * SIGS + (SIG_GB + 6 + 2 * n))
                    else:
                        pe.wait_ge(ret_gated, l * 8 + (n - 1))
                    for p in range(2):
                        u = U_RET + 3 * n + 1 + p
                        unit(l, u // RING, u % RING, g + 1, tile_of(ghi, glo), k0=8 * p, start=(p == 0), stop=(p == 1),
                             ready=(lambda k: pe.wait_ge(g_ready, l * 7 + (k // 4 + 1 if k < 12 else k - 8))) if n == 0 else None)
                    if n == 1:
                        pe.wait_ge(conv_step, l * (KT * CONVS) + KT * CONVS)
                        pe.wait_ge(sample_conv_step, l * (2 * TAPS) + 2 * TAPS)
                        pe.wait_ge(conv_sum, l * 6 + 3)
                        pe.matmul(X[:, 0:T], ones_d[:, :], csum[:, 0, :], start=True, stop=True).then_inc(stat_done, 1)
                    if n == 4:
                        pe.wait_ge(stat_read, l * STATS + (ST_CMEAN + 1))
                        pe.wait_ge(conv_sum, l * 6 + 6)
                        pe.matmul(X[:, 0:T], ones_d[:, :], sqz[:, 0, :], start=True, stop=True).then_inc(stat_done, 1)
                for n in range(KT):
                    if n < 4:
                        if n % 2 == 0:
                            pe.wait_ge(sig_done, l * SIGS + (SIG_GA + 7 + n // 2))
                        else:
                            pe.wait_ge(ret_gated, l * 8 + (7 + n // 2))
                    else:
                        pe.wait_ge(merge_step, l * 16 + (2 * (n - 4) + 1))
                    u = U_CO + n
                    unit(l, u // RING, u % RING, n % 4, tile_of(zhi, zlo),
                         ready=(lambda k: pe.wait_ge(z_ready, l * 8 + (k + 1))) if n == 0 else None)
                pe.wait_ge(stat_read, l * STATS + (ST_CVAR + 1))
                for n in range(KT):
                    if n < 4:
                        pe.wait_ge(merge_step, l * 16 + (2 * (n + 4) + 1))
                    else:
                        pe.wait_ge(y_copied, l * 16 + (n - 3))
                    u = U_WO + n
                    unit(l, u // RING, u % RING, n % 4, h_tile,
                         ready=(lambda k: pe.wait_ge(m_ready, l * 8 + (k + 1))) if n == 0 else None,
                         between=(lambda k: square_mean(l, SQ_POST, n - 1) if k == 4 else None) if n else None)
                square_mean(l, SQ_POST, KT - 1).then_inc(stat_done, 1)
                keep_clock(20)
                pe.wait_ge(stat_read, l * STATS + (ST_POST + 1))
                for k in range(KT):
                    mean = square_mean(l, SQ_FFN, k)
                mean.then_inc(stat_done, 1)
                keep_clock(20)
                first_units(l, U_GU // RING, lambda k: h_read(l, 8 + k))
                unit(l, U_GU // RING, AHEAD, AHEAD, h_tile)
                with pe.Fori(1, FT // 2) as i:
                    for j in range(4):
                        pe.wait_ge(ffn_step, l * (2 * FT) + i * 4 + (j - 3))
                        unit(l, i + U_GU // RING, j, j, h_tile)
                pe.wait_ge(stat_read, l * STATS + (ST_FFN + 1))
                for n in range(KT):
                    if n < 4:
                        pe.wait_ge(ffn_step, l * (2 * FT) + (2 * FT - 3 + n))
                    else:
                        pe.wait_ge(y_copied, l * 16 + (8 + n - 3))
                    for p in range(3):
                        u = U_DOWN + 3 * n + p
                        unit(l, u // RING, u % RING, n % 4, tile_of(fhi, flo), k0=8 * p, n=min(8, FT - 8 * p),
                             start=(p == 0), stop=(p == 2),
                             ready=(lambda k: pe.wait_ge(f_ready, l * FT + (k + 1))) if n == 0 else None,
                             between=(lambda k: square_mean(l, SQ_POST2, n - 1) if k == 4 else None) if n and p == 0 else None)
                square_mean(l, SQ_POST2, KT - 1).then_inc(stat_done, 1)
                keep_clock(20)

        @block.scalar
        def _(act):
            def split(l, u, i=0):
                v = u + AHEAD
                s = v % RING
                act.wait_ge(w_ready[s], l * (UNITS // RING * 16) + i * 16 + (v // RING + 1) * 16)
                if v >= RING:
                    act.wait_ge(unit_done, l * UNITS + i * RING + (v + 1 - RING))
                act.activation(whi[s][:, :, :], wring[s][:, :, :], ACT.Copy).then_inc(hi_done, 1)

            def gemm(l, u):
                act.wait_ge(unit_done, l * UNITS + (u + 1))

            def log_table(l, rs):
                if not (isinstance(rs, int) and rs == 0):
                    act.wait_ge(rstd_done, l * RSTDS + rs)
                act.activation(lnv[:, 0:1], eps[:, 0:1], ACT.Ln).then_inc(log_loaded, 1)

            def rsqrt(l, src, st, rs, aux_read=None):
                act.wait_ge(log_loaded, l * RSTDS + rs + 1)
                ln = act.activation(lnv[:, :], src, ACT.Ln, bias=eps[:, 0:1])
                if aux_read is None:
                    ln.then_inc(stat_read, 1)
                    act.wait_ge(stat_read, l * STATS + (st + 1))
                else:
                    ln.then_inc(act_aux, 1)
                    act.wait_ge(act_aux, aux_read)
                act.activation(rstd[:, :], lnv[:, :], ACT.Exp, scale=-0.5).then_inc(rstd_done, 1)

            def split_head(l, hd, j):
                v = j + AHEAD
                s = v % RING
                act.wait_ge(w_ready[s], l * (UNITS // RING * 16) + hd * (HEAD_UNITS // RING * 16) + ((U_HEAD + v) // RING + 1) * 16)
                act.wait_ge(unit_done, l * UNITS + hd * HEAD_UNITS + (U_HEAD + v + 1 - RING))
                act.activation(whi[s][:, :, :], wring[s][:, :, :], ACT.Copy).then_inc(hi_done, 1)

            def sigmoid(dst, src, bias=None):
                if bias is None:
                    act.activation(dst, src, ACT.Sigmoid).then_inc(sig_done, 1)
                else:
                    act.activation(dst, src, ACT.Sigmoid, bias=bias).then_inc(sig_done, 1)

            def late(l, hd, j):
                H = l * HEADS + hd
                if j == 0:
                    for p in range(2):
                        act.wait_ge(aux_done, H * AUX_HEAD + (A_P + p + 1))
                        act.activation(oT[:, 2 * p:2 * p + 2, 0:SEQ], aux[(A_P + p) % 3][:, :].rearrange("p (e t) -> p e t", e=2),
                                       ACT.Copy).then_inc(act_aux, 1)
                if j == 5:
                    act.wait_ge(stat_done, l * STATS + (hd + (ST_X + 1)))
                    act.activation(oT[:, :, SEQ:T], X[:, 0:256].rearrange("p (e t) -> p e t", e=4), ACT.Copy).then_inc(stat_read, 1)
                if j == 5:
                    for d in range(2):
                        act.wait_ge(aux_done, H * AUX_HEAD + (A_PU + d + 1))
                        act.activation(pst[:, d, :], aux[(A_PU + d) % 3][:, :], ACT.Copy).then_inc(act_aux, 1)
                if j == 6:
                    act.wait_ge(dve_aux, H * AUX_DVE + 20)
                    act.activation(sqo[:, :, :], oT[:, :, :], ACT.Square).then_inc(sq_done, 1)
                if j == 8:
                    act.wait_ge(aux_done, H * AUX_HEAD + (A_VAR + 1))
                    rsqrt(l, aux[A_VAR % 3][:, 0:T], None, hd + RS_RET, aux_read=H * AUX_ACT + 8)

            def head(l, hd, first):
                H = l * HEADS + hd
                for j in range(HEAD_UNITS):
                    split_head(l, hd, j)
                    if not first and j < 8:
                        late(l, hd - 1, j)
                    if not first and j == 6:
                        log_table(l, hd - 1 + RS_RET)
                    if 4 <= j < 8:
                        if j == 4 and not first:
                            act.wait_ge(aux_done, H * AUX_HEAD + (A_V + 3 - AUX_HEAD))
                        act.wait_ge(unit_done, l * UNITS + hd * HEAD_UNITS + (U_HEAD + j + 1))
                        act.activation(qkv[:, j, :], bank[j % 4][:, 0:T], ACT.Copy).then_inc(v_copied, 1)
                    if j == 8 and not first:
                        late(l, hd - 1, 8)
                    if j == 8:
                        act.wait_ge(rope_step, H * ROPES + ROPES)
                        act.wait_ge(v_copied, H * 4 + 4)
                        for buf, t0, n in ((kdup, 2, 2), (vdup, 4, 4)):
                            src = qkv[:, t0:t0 + n, SEQ:T].rearrange("p d (o t) -> p d o t", o=1).to_broadcast([P, n, 2, T - SEQ])
                            act.activation(buf[:, :, :].rearrange("p d (o t) -> p d o t", o=2), src, ACT.Copy).then_inc(dup_ready, 1)
                    if j == 9:
                        act.wait_ge(aux_done, H * AUX_HEAD + (A_KTS + 1))
                        act.activation(kd[:, :], aux[1][:, 0:DK], ACT.Copy, scale=con[:, ds(hd + C_KROW, 1)]).then_inc(act_aux, 1)
                        act.wait_ge(act_aux, H * AUX_ACT + 1)
                        act.activation(khl[:, :], kd[:, :], ACT.Copy).then_inc(kd_ready, 1)
                    if j >= 8:
                        if first:
                            act.wait_ge(u_ready, l * 16 + (2 * (j - 4) + 2))
                        else:
                            act.wait_ge(sg_ready, H * 4 + (j - 7 - 4))
                        act.wait_ge(unit_done, l * UNITS + hd * HEAD_UNITS + (U_HEAD + j + 1))
                        sigmoid(sig[:, j - 8, :], bank[j % 4][:, 0:T])
                    if j >= 10:
                        for c in ((0, 1), (2,))[j - 10]:
                            n = P if c < 2 else T - SEQ
                            act.wait_ge(aux_done, H * AUX_HEAD + (A_V + c + 1))
                            act.activation(vtok[0:n, c, :], aux[(A_V + c) % 3][0:n, :], ACT.Copy).then_inc(act_aux if c < 2 else vs_hi, 1)
                            if c == 2:
                                act.activation(vshi[:, :], aux[(A_V + c) % 3][:, :], ACT.Copy).then_inc(vs_hi, 1)
                if not first:
                    act.wait_ge(ret_norm, H * 6)
                    act.wait_ge(pst_stored, H * 16)

            def squares_of_products(l, u0, ustep, sq0):
                for n in range(KT):
                    for p in range(ustep):
                        split(l, u0 + ustep * n + p)
                    act.wait_ge(unit_done, l * UNITS + (u0 + ustep * n + ustep))
                    act.activation(sq8[:, n, :], bank[n % 4][:, 0:T], ACT.Square).then_inc(sq_done, 1)

            def halves_of_h(l, sub):
                for k in range(KT):
                    act.wait_ge(h_value, l * 16 + (8 * sub + k + 1))
                    act.activation(hhi[:, k, :], acc[:, k, :], ACT.Copy).then_inc(h_hi, 1)

            act.wait_ge(x_loaded, 16)
            for k in range(KT):
                act.activation(sq8[:, k, :], x[:, k, :], ACT.Square).then_inc(sq_done, 1)
            act.wait_ge(memset_done, 3)
            log_table(0, 0)
            def merged_half(l, n):
                act.wait_ge(merge_step, l * 16 + (2 * n + 2))
                act.activation(hhi[:, n, :], acc2[:, n, :], ACT.Copy).then_inc(m_hi, 1)

            def half_of_z(l, k):
                act.wait_ge(conv_norm, l * 24 + (16 + k + 1))
                act.activation(zhi[:, k, :], acc[:, k, :], ACT.Copy).then_inc(z_hi, 1)

            for s in range(AHEAD):
                act.wait_ge(w_ready[s], 16)
                act.activation(whi[s][:, :, :], wring[s][:, :, :], ACT.Copy).then_inc(hi_done, 1)
            with act.Fori(0, DEPTH) as l:
                act.wait_ge(stat_done, l * STATS + 1)
                rsqrt(l, X[:, 0:T], 0, 0)
                halves_of_h(l, 0)
                for n in range(KT):
                    split(l, U_CIN + 2 * n)
                    if n >= 4:
                        act.wait_ge(u_ready, l * 16 + (2 * (n - 4) + 2))
                    gemm(l, U_CIN + 2 * n)
                    sigmoid(sig[:, n % 4, :], bank[(2 * n) % 4][:, 0:T])
                    split(l, U_CIN + 2 * n + 1)
                head(l, 0, True)
                with act.Fori(1, HEADS) as hd:
                    head(l, hd, False)
                act.wait_ge(aux_done, (l * HEADS + (HEADS - 1)) * AUX_HEAD + (A_S + 1))
                act.wait_ge(qd_ready, l * HEADS + HEADS)
                for n in range(KT):
                    split(l, U_GB + n)
                    late(l, HEADS - 1, n)
                    gemm(l, U_GB + n)
                    sigmoid(sgb[:, n, :], bank[n % 4][:, 0:T], bias=g_(G_GATE + 8 + n))
                    if n >= 5:
                        c = n - 5
                        act.wait_ge(ret_norm, l * (HEADS * 6) + 6 * (c + 1))
                        act.activation(ghi[:, 4 * c:4 * c + 4, :], go[:, 4 * c:4 * c + 4, :], ACT.Copy).then_inc(g_hi, 1)
                log_table(l, HEADS - 1 + RS_RET)
                late(l, HEADS - 1, 8)
                act.wait_ge(pst_stored, l * (HEADS * 16) + HEADS * 16)
                for j in range(4):
                    act.wait_ge(ret_norm, l * (HEADS * 6) + ((HEADS - 1) * 6 + 3 * (j // 2 + 1)))
                    act.activation(ghi[:, 12 + j, :], go[:, 12 + j, :], ACT.Copy).then_inc(g_hi, 1)
                for n in range(KT):
                    split(l, U_RET + 3 * n)
                    if n < 4:
                        act.wait_ge(sg_ready, l * 16 + (12 + n + 1))
                    else:
                        act.wait_ge(ret_gated, l * 8 + (n - 3))
                    gemm(l, U_RET + 3 * n)
                    sigmoid(sig[:, n % 4, :], bank[(2 * n) % 4][:, 0:T], bias=g_(G_GATE + n))
                    split(l, U_RET + 3 * n + 1)
                    split(l, U_RET + 3 * n + 2)
                    if n == 2:
                        act.wait_ge(stat_done, l * STATS + (ST_CMEAN + 1))
                        act.activation(cmean[:, :], X[:, 0:T], ACT.Copy).then_inc(stat_read, 1)
                    if n == 3:
                        act.wait_ge(g_ready, l * 7 + 7)
                        for k in range(KT):
                            act.wait_ge(conv_norm, l * 24 + (k + 1))
                            act.activation(sqz[:, k, :], acc[:, k, :], ACT.Square).then_inc(sq_done, 1)
                    if n == 5:
                        log_table(l, RS_CONV)
                        act.wait_ge(stat_done, l * STATS + (ST_CVAR + 1))
                        rsqrt(l, X[:, 0:T], ST_CVAR, RS_CONV)
                    if n >= 6:
                        for k in range(4 * (n - 6), 4 * (n - 6) + 4):
                            act.wait_ge(conv_norm, l * 24 + (8 + k + 1))
                            if k >= 4:
                                act.wait_ge(conv_norm, l * 24 + (16 + k - 3))
                            act.activation(tmp[:, k % 4, :], acc[:, k, :], ACT.Sigmoid, bias=g_(G_LNB + k)).then_inc(zsig_done, 1)
                            if k:
                                half_of_z(l, k - 1)
                half_of_z(l, KT - 1)
                for n in range(KT):
                    split(l, U_CO + n)
                    if n:
                        merged_half(l, n - 1)
                merged_half(l, KT - 1)
                log_table(l, RS_POST)
                squares_of_products(l, U_WO, 1, SQ_POST)
                act.wait_ge(stat_done, l * STATS + (ST_POST + 1))
                rsqrt(l, X[:, 0:T], ST_POST, RS_POST)
                log_table(l, RS_FFN)
                for k in range(KT):
                    act.wait_ge(post_step, l * POSTS + (k // 2 * 2 + 2))
                    act.activation(sq8[:, k, :], x[:, k, :], ACT.Square).then_inc(sq_done, 1)
                act.wait_ge(stat_done, l * STATS + (ST_FFN + 1))
                rsqrt(l, X[:, 0:T], ST_FFN, RS_FFN)
                halves_of_h(l, 1)

                def f_half(n, slot):
                    act.wait_ge(ffn_step, l * (2 * FT) + 2 * n + 2)
                    act.activation(fhi[:, ds(n, 1), :].rearrange("p o t -> p (o t)"), tmp[:, slot, :], ACT.Copy).then_inc(f_hi, 1)

                def gates(i, first):
                    for j in range(2):
                        split(l, U_GU + 2 * j, i)
                        if not first:
                            act.wait_ge(ffn_step, l * (2 * FT) + i * 4 + (2 * j - 3))
                        act.wait_ge(unit_done, l * UNITS + i * RING + (U_GU + 2 * j + 1))
                        sigmoid(sig[:, j, :], bank[2 * j][:, 0:T])
                        if j or not first:
                            f_half(i * 2 + (j - 1), 1 - j)
                        split(l, U_GU + 2 * j + 1, i)

                gates(0, True)
                with act.Fori(1, FT // 2) as i:
                    gates(i, False)
                f_half(FT - 1, 1)
                log_table(l, RS_POST2)
                squares_of_products(l, U_DOWN, 3, SQ_POST2)
                act.wait_ge(stat_done, l * STATS + (ST_POST2 + 1))
                rsqrt(l, X[:, 0:T], ST_POST2, RS_POST2)
                log_table(l, RSTDS)
                for k in range(KT):
                    act.wait_ge(post_step, l * POSTS + (8 + k // 2 * 2 + 2))
                    act.activation(sq8[:, k, :], x[:, k, :], ACT.Square).then_inc(sq_done, 1)

        @block.vector
        def _(dve):
            def lower(dst, value, hi):
                return dve.tensor_tensor(dst, value, hi.bitcast(F32), ALU.subtract)

            def split(l, u, hd=0, i=0):
                v = u + AHEAD
                s = v % RING
                if isinstance(hd, int):
                    dve.wait_ge(hi_done, l * UNITS + i * RING + (v + 1 + hd * HEAD_UNITS))
                else:
                    dve.wait_ge(hi_done, l * UNITS + hd * HEAD_UNITS + (v + 1))
                lower(wlo[s][:, :, :], wring[s][:, :, :], whi[s][:, :, :]).then_inc(lo_done, 1)

            def normalised(l, sub, rs, gain):
                dve.wait_ge(rstd_done, l * RSTDS + (rs + 1))
                for k in range(KT + 2):
                    if k < KT:
                        dve.scalar_tensor_tensor(out=acc[:, k, :], in0=x[:, k, :], scalar=g_(gain + k), in1=rstd[:, :],
                                                 op0=ALU.mult, op1=ALU.mult).then_inc(h_value, 1)
                    if k >= 2:
                        dve.wait_ge(h_hi, l * 16 + (8 * sub + k - 1))
                        lower(hlo[:, k - 2, :], acc[:, k - 2, :], hhi[:, k - 2, :]).then_inc(h_ready, 1)

            def conv_tap(l, pair, k):
                for i in range(2):
                    n = pair * 2 + i
                    tap = par[:, ds(n * TAPS + (G_CW + k), 1)]
                    out = acc[:, ds(n, 1), 0:SEQ].rearrange("p o t -> p (o t)")
                    src = up[:, ds(n, 1), k:k + SEQ].rearrange("p o t -> p (o t)")
                    if k == 0:
                        dve.tensor_scalar(out, src, tap, par[:, ds(n + G_CB, 1)], ALU.mult, ALU.add).then_inc(conv_step, 1)
                    else:
                        dve.wait_ge(conv_step, l * (KT * CONVS) + pair * (2 * CONVS) + (2 * (k - 1) + i + 1))
                        dve.scalar_tensor_tensor(out=out, in0=src, scalar=tap, in1=out, op0=ALU.mult, op1=ALU.add).then_inc(conv_step, 1)

            def conv_taps(l, pair, a, b):
                for k in range(a, b):
                    conv_tap(l, pair, k)

            def rope(l, hd, i, first):
                H = l * HEADS + hd
                base = H * ROPES + 6 * i
                x1, x2 = bank[2 * i][:, 0:T], bank[2 * i + 1][:, 0:T]
                dve.wait_ge(unit_done, l * UNITS + hd * HEAD_UNITS + (U_HEAD + 2 * i + 2))
                if i == 1:
                    dve.wait_ge(rope_step, base)
                cos, sin = col(C_COS, T), col(C_SIN, T)
                for n, (a, b) in enumerate(((x1, cos), (x2, sin), (x1, sin), (x2, cos))):
                    dve.tensor_tensor(tmp[:, n, :], a, b, ALU.mult).then_inc(rope_step, 1)
                dve.wait_ge(rope_step, base + 2)
                dve.tensor_tensor(qkv[:, 2 * i, :], tmp[:, 0, :], tmp[:, 1, :], ALU.subtract).then_inc(rope_step, 1)
                dve.wait_ge(rope_step, base + 4)
                dve.tensor_tensor(qkv[:, 2 * i + 1, :], tmp[:, 2, :], tmp[:, 3, :], ALU.add).then_inc(rope_step, 1)

            def update(l, hd, b, d):
                pos = A_U + 2 * b + d
                dve.wait_ge(aux_done, (l * HEADS + hd) * AUX_HEAD + (pos + 1))
                st = state[b % RING][:, d, :]
                dve.scalar_tensor_tensor(out=st, in0=st, scalar=con[:, ds(hd + C_CD, 1)], in1=aux[pos % 3][:, :],
                                         op0=ALU.mult, op1=ALU.add).then_inc(dve_aux, 1)

            def centre(l, hd):
                H = l * HEADS + hd
                dve.wait_ge(aux_done, H * AUX_HEAD + (A_MEAN + 1))
                mean = aux[A_MEAN % 3][:, 0:T].rearrange("p (o t) -> p o t", o=1).to_broadcast([P, 4, T])
                dve.tensor_tensor(oT[:, :, :], oT[:, :, :], mean, ALU.subtract).then_inc(dve_aux, 1)

            def normalise(l, hd, last=False):
                H = l * HEADS + hd
                dve.wait_ge(rope_step, (H + (1 if last else 2)) * ROPES)
                dve.wait_ge(dve_aux, H * AUX_DVE + 20)
                dve.wait_ge(rstd_done, l * RSTDS + (hd + (RS_RET + 1)))
                dve.wait_ge(sg_ready, H * 4 + 4)
                for e in range(0, 4, 2):
                    for i in (e, e + 1):
                        dve.scalar_tensor_tensor(out=tmp[:, i, :], in0=oT[:, i, :], scalar=par[:, ds(hd * 4 + (G_RET + i), 1)],
                                                 in1=rstd[:, :], op0=ALU.mult, op1=ALU.mult).then_inc(ret_norm, 1)
                    dve.wait_ge(ret_norm, H * 6 + (e // 2 * 3 + 2))
                    dve.tensor_tensor(go[:, ds(hd * 4 + e, 2), :], tmp[:, e:e + 2, :], sg[:, e:e + 2, :], ALU.mult).then_inc(ret_norm, 1)

            def gate(l, hd, j, first):
                if j == 0 and not first:
                    dve.wait_ge(ret_norm, (l * HEADS + hd) * 6)
                dve.wait_ge(sig_done, l * SIGS + hd * 4 + (SIG_G + j + 1))
                dve.tensor_tensor(sg[:, j, :], bank[j][:, 0:T], sig[:, j, :], ALU.mult).then_inc(sg_ready, 1)

            def decayed_keys(l, hd):
                H = l * HEADS + hd
                dve.wait_ge(aux_done, H * AUX_HEAD + (A_KT + 1))
                dec = con[:, ds(hd * 2 + C_KDEC, 2)].rearrange("p (c o) -> p c o", o=1).to_broadcast([P, 2, DK])
                dve.tensor_tensor(kdec[:, :, :], aux[0][:, :].rearrange("p (c d) -> p c d", c=2), dec, ALU.mult).then_inc(dve_aux, 1)
                dve.wait_ge(kd_ready, H + 1)
                lower(khl[64:P, :], kd[64:P, :], khl[64:P, :]).then_inc(khl_step, 1)
                dve.wait_ge(khl_step, H + 1)
                own = con[:, C_OWN:C_OWN + DB].rearrange("p (b o) -> p b o", o=1).to_broadcast([P, DB, DK])
                src = khl[:, :].bitcast(F32).rearrange("p (o d) -> p o d", o=1).to_broadcast([P, DB, DK])
                dve.tensor_tensor(kdecs[:, :, :], src, own, ALU.mult).then_inc(ks_ready, 1)

            def values_low(l, hd):
                H = l * HEADS + hd
                dve.wait_ge(vs_hi, H * 2 + 2)
                lower(vslo[:, :], aux[(A_V + 2) % 3][:, :], vshi[:, :]).then_inc(dve_aux, 1)

            def decayed_queries(l, hd, first):
                dve.wait_ge(rope_step, (l * HEADS + hd) * ROPES + ROPES)
                if not first:
                    dve.wait_ge(stat_done, l * STATS + (hd + ST_X))
                dve.tensor_tensor(qd[:, :, :], qkv[:, 0:2, SEQ:T],
                                  con[:, ds(hd * 64 + C_QDEC, 64)].rearrange("p (o t) -> p o t", o=1).to_broadcast([P, 2, 64]),
                                  ALU.mult).then_inc(qd_ready, 1)

            def masked_scores(l, hd):
                dve.wait_ge(aux_done, (l * HEADS + hd) * AUX_HEAD + (A_S + 1))
                b = aux[A_S % 3]
                dve.tensor_tensor(stm[0:64, SEQ + P:MASKW], b[0:64, SEQ + P:MASKW], con[0:64, ds(hd * MASKW + (C_MASK + SEQ + P), 64)],
                                  ALU.mult).then_inc(sample_masked, 1)
                dve.tensor_tensor(stm[:, 0:SEQ + P], b[:, 0:SEQ + P], con[:, ds(hd * MASKW + C_MASK, SEQ + P)], ALU.mult).then_inc(dve_aux, 1)

            def head(l, hd, first):
                taps = (2, 1, 2, 1, 2, 1, 1, 1, 1, 0, 0, 1) if first else (5, 2, 4, 2, 4, 6, 3, 4, 1, 0, 0, 0)
                for j in range(HEAD_UNITS):
                    split(l, U_HEAD + j, hd)
                    t0 = 18 if first else 0
                    t = t0 + sum(taps[:j])
                    if not first and 1 <= j <= 4:
                        for i in range(4):
                            conv_taps(l, hd, t, t + (i < taps[j]))
                            t += i < taps[j]
                            update(l, hd - 1, 2 * (j - 1) + i // 2, i % 2)
                    conv_taps(l, hd, t, t0 + sum(taps[:j + 1]))
                    if j == 1 or j == 3:
                        rope(l, hd, j // 2, first)
                    if j == 5 and not first:
                        centre(l, hd - 1)
                    if j == 9:
                        decayed_keys(l, hd)
                        masked_scores(l, hd)
                        if not first:
                            normalise(l, hd - 1)
                        gate(l, hd, 0, first)
                    if j >= 9:
                        gate(l, hd, j - 8, first)
                        if j == 10:
                            decayed_queries(l, hd, first)
                values_low(l, hd)

            dve.memset(ones_d[:, :], 1.0 / D).then_inc(memset_done, 1)
            dve.memset(ones_v[:, :], 1.0 / DV).then_inc(memset_done, 1)
            dve.memset(eps[:, :], EPS).then_inc(memset_done, 1)
            for s in range(AHEAD):
                dve.wait_ge(hi_done, s + 1)
                lower(wlo[s][:, :, :], wring[s][:, :, :], whi[s][:, :, :]).then_inc(lo_done, 1)
            with dve.Fori(0, DEPTH) as l:
                dve.wait_ge(par_loaded, l * 16 + 16)
                normalised(l, 0, 0, G_MIXPRE)
                dve.memset(up[:, :, 0:PAD], 0.0).then_inc(pad_zeroed, 1)
                dve.wait_ge(u_loaded, l * 16 + 16)
                dve.wait_ge(pad_zeroed, l + 1)
                for n in range(KT):
                    split(l, U_CIN + 2 * n)
                    split(l, U_CIN + 2 * n + 1)
                    dve.wait_ge(unit_done, l * UNITS + (U_CIN + 2 * n + 2))
                    dve.wait_ge(sig_done, l * SIGS + (n + 1))
                    b, s = bank[(2 * n + 1) % 4], sig[:, n % 4, :]
                    dve.tensor_tensor(up[:, n, PAD:PAD + SEQ], b[:, 0:SEQ], s[:, 0:SEQ], ALU.mult).then_inc(u_ready, 1)
                    dve.tensor_tensor(us[:, n, :, PAD:PAD + DS], b[:, SEQ:T].rearrange("p (b t) -> p b t", b=DB),
                                      s[:, SEQ:T].rearrange("p (b t) -> p b t", b=DB), ALU.mult).then_inc(u_ready, 1)
                    if n >= 2:
                        dve.wait_ge(u_ready, l * 16 + 4)
                        conv_taps(l, 0, 3 * (n - 2), 3 * (n - 1))
                dve.wait_ge(u_ready, l * 16 + 16)
                dve.wait_ge(con_loaded, 16)
                head(l, 0, True)
                with dve.Fori(1, HEADS) as hd:
                    head(l, hd, False)
                last = HEADS - 1

                def gated_low(c):
                    dve.wait_ge(g_hi, l * 7 + (c + 1))
                    lower(glo[:, 4 * c:4 * c + 4, :], go[:, 4 * c:4 * c + 4, :], ghi[:, 4 * c:4 * c + 4, :]).then_inc(g_ready, 1)

                for n in range(KT):
                    split(l, U_GB + n)
                    if 1 <= n <= 4:
                        for i in range(4):
                            update(l, last, 2 * (n - 1) + i // 2, i % 2)
                    if n == 5:
                        centre(l, last)
                    if n == 6:
                        dve.wait_ge(pst_stored, l * (HEADS * 16) + HEADS * 16)
                        for s in range(RING):
                            dve.wait_ge(r_stored[s], l * (HEADS * 32) + HEADS * 32)
                        gated_low(0)
                    if n == 7:
                        gated_low(1)
                        gated_low(2)
                dve.wait_ge(sample_conv_step, l * (2 * TAPS) + 2 * TAPS)
                normalise(l, last, True)
                for j in range(4):
                    dve.wait_ge(g_hi, l * 7 + (3 + j + 1))
                    lower(glo[:, 12 + j, :], go[:, 12 + j, :], ghi[:, 12 + j, :]).then_inc(g_ready, 1)
                def z_low(k):
                    dve.wait_ge(z_hi, l * 8 + (k + 1))
                    lower(zlo[:, k, :], acc[:, k, :], zhi[:, k, :]).then_inc(z_ready, 1)

                dve.wait_ge(u_saved, l * 32 + 32)
                dve.wait_ge(conv_step, l * (KT * CONVS) + KT * CONVS)
                dve.wait_ge(sample_conv_step, l * (2 * TAPS) + 2 * TAPS)
                for n in range(KT):
                    for p in range(3):
                        split(l, U_RET + 3 * n + p)
                    dve.wait_ge(sig_done, l * SIGS + (SIG_GA + n + 1))
                    dve.wait_ge(unit_done, l * UNITS + (U_RET + 3 * n + 3))
                    dve.tensor_tensor(acc2[:, n, :], bank[(2 * n + 1) % 4][:, 0:T], sig[:, n % 4, :], ALU.mult).then_inc(ret_gated, 1)
                    if n == 2:
                        dve.wait_ge(stat_read, l * STATS + (ST_CMEAN + 1))
                        for k in range(KT):
                            dve.tensor_tensor(acc[:, k, :], acc[:, k, :], cmean[:, :], ALU.subtract).then_inc(conv_norm, 1)
                    if n >= 6:
                        for k in range(4 * (n - 6), 4 * (n - 6) + 4):
                            dve.wait_ge(zsig_done, l * 8 + (k + 1))
                            dve.wait_ge(conv_norm, l * 24 + (8 + k + 1))
                            dve.scalar_tensor_tensor(out=acc[:, k, :], in0=acc[:, k, :], scalar=g_(G_LNB + k), in1=tmp[:, k % 4, :],
                                                     op0=ALU.add, op1=ALU.mult).then_inc(conv_norm, 1)
                            if k >= 2:
                                z_low(k - 2)
                    if n == 5:
                        dve.wait_ge(conv_norm, l * 24 + 8)
                        dve.wait_ge(rstd_done, l * RSTDS + (RS_CONV + 1))
                        for k in range(KT):
                            dve.scalar_tensor_tensor(out=acc[:, k, :], in0=acc[:, k, :], scalar=g_(G_LNG + k), in1=rstd[:, :],
                                                     op0=ALU.mult, op1=ALU.mult).then_inc(conv_norm, 1)
                for k in range(KT - 2, KT):
                    z_low(k)

                def merged_low(n):
                    dve.wait_ge(m_hi, l * 8 + (n + 1))
                    lower(hlo[:, n, :], acc2[:, n, :], hhi[:, n, :]).then_inc(m_ready, 1)

                for n in range(KT):
                    split(l, U_CO + n)
                    dve.wait_ge(unit_done, l * UNITS + (U_CO + n + 1))
                    dve.wait_ge(sig_done, l * SIGS + (SIG_GB + n + 1))
                    dve.tensor_tensor(tmp[:, n % 4, :], bank[n % 4][:, 0:T], sgb[:, n, :], ALU.mult).then_inc(merge_step, 1)
                    dve.wait_ge(merge_step, l * 16 + (2 * n + 1))
                    dve.wait_ge(ret_gated, l * 8 + (n + 1))
                    dve.tensor_tensor(acc2[:, n, :], acc2[:, n, :], tmp[:, n % 4, :], ALU.add).then_inc(merge_step, 1)
                    if n:
                        merged_low(n - 1)
                merged_low(KT - 1)

                def post(sub, rs, sq0, gain, u0, ustep):
                    for n in range(KT):
                        for p in range(ustep):
                            split(l, u0 + ustep * n + p)
                        dve.wait_ge(sq_done, l * SQS + (sq0 + n + 1))
                        dve.tensor_scalar(acc[:, n, :], bank[n % 4][:, 0:T], g_(gain + n), None, ALU.mult).then_inc(y_copied, 1)
                    dve.wait_ge(rstd_done, l * RSTDS + (rs + 1))
                    dve.wait_ge(y_copied, l * 16 + (8 * sub + 8))
                    scale = rstd[:, :].rearrange("p (o t) -> p o t", o=1).to_broadcast([P, 2, T])
                    for n in range(0, KT, 2):
                        y = tmp[:, n % 4:n % 4 + 2, :]
                        dve.tensor_tensor(y, acc[:, n:n + 2, :], scale, ALU.mult).then_inc(post_step, 1)
                        dve.wait_ge(post_step, l * POSTS + (8 * sub + n + 1))
                        dve.tensor_tensor(x[:, n:n + 2, :], x[:, n:n + 2, :], y, ALU.add).then_inc(post_step, 1)

                post(0, RS_POST, SQ_POST, G_MIXPOST, U_WO, 1)
                dve.wait_ge(post_step, l * POSTS + 8)
                normalised(l, 1, RS_FFN, G_FFNPRE)

                def ffn_low(n, slot):
                    dve.wait_ge(f_hi, l * FT + n + 1)
                    lower(flo[:, ds(n, 1), :].rearrange("p o t -> p (o t)"), tmp[:, slot, :],
                          fhi[:, ds(n, 1), :].rearrange("p o t -> p (o t)")).then_inc(f_ready, 1)

                def hidden(i, first):
                    for j in range(2):
                        split(l, U_GU + 2 * j, i=i)
                        dve.wait_ge(sig_done, l * SIGS + i * 2 + (SIG_GATE + j + 1))
                        if not first:
                            dve.wait_ge(f_ready, l * FT + i * 2 + (j - 1))
                        dve.tensor_tensor(tmp[:, j, :], bank[2 * j][:, 0:T], sig[:, j, :], ALU.mult).then_inc(ffn_step, 1)
                        if j or not first:
                            ffn_low(i * 2 + (j - 1), 1 - j)
                        split(l, U_GU + 2 * j + 1, i=i)
                        dve.wait_ge(ffn_step, l * (2 * FT) + i * 4 + (2 * j + 1))
                        dve.wait_ge(unit_done, l * UNITS + i * RING + (U_GU + 2 * j + 2))
                        dve.tensor_tensor(tmp[:, j, :], bank[2 * j + 1][:, 0:T], tmp[:, j, :], ALU.mult).then_inc(ffn_step, 1)

                hidden(0, True)
                with dve.Fori(1, FT // 2) as i:
                    hidden(i, False)
                ffn_low(FT - 1, 1)
                post(1, RS_POST2, SQ_POST2, G_FFNPOST, U_DOWN, 3)
                dve.wait_ge(post_step, l * POSTS + 16)


def constants():
    c = np.zeros((P, NCONST), np.float32)
    half = DK // 2
    freqs = (np.float32(10000.0) ** (-np.arange(half, dtype=np.float32) / np.float32(half))).astype(np.float32)
    pos = np.concatenate([np.arange(SEQ), np.tile(PAST + np.arange(DS), DB)]).astype(np.float32)
    ang = (pos[None, :] * freqs[:, None]).astype(np.float32).astype(np.float64)
    c[:, C_COS:C_COS + T], c[:, C_SIN:C_SIN + T] = np.cos(ang), np.sin(ang)
    scale = DK ** -0.5
    p = np.arange(P)
    for h in range(HEADS):
        g = float(np.log1p(-np.exp2(-5.0 - h)))
        j, i = p[:, None], np.arange(SEQ)[None, :]
        m = np.where(i >= j, np.exp(g * np.maximum(i - j, 0)), 0.0) * scale
        o = C_MASK + h * MASKW
        c[:, o:o + SEQ], c[:, o + SEQ:o + SEQ + P] = m, m[:, :P]
        j, i = p[:64, None], p[None, :64]
        c[:64, o + SEQ + P:o + MASKW] = np.where((i // DS == j // DS) & (i >= j), np.exp(g * np.maximum(i - j, 0)), 0.0) * scale
        c[:, C_KDEC + 2 * h] = np.exp(g * (SEQ - 1 - p)) * scale
        c[:, C_KDEC + 2 * h + 1] = np.exp(g * (P - 1 - p)) * scale
        c[:, C_KROW + h] = np.exp(g * (DS - 1 - p % DS)) * scale
        c[:, C_QDEC + 64 * h:C_QDEC + 64 * (h + 1)] = np.exp(g * (p[:64] % DS + 1.0))
        c[:, C_CD + h] = math.exp(g * DS)
    c[:, C_OWN:C_OWN + DB] = p[:, None] % (DB * DS) // DS == np.arange(DB)
    c[:, C_ID:C_ID + P] = np.eye(P)
    return c


def units_of(w_in, w_ret_out, w_conv_out, w_o, w_gate, w_up, w_down):
    def tiles(w):
        k, n = w.shape
        t = w.reshape(k // P, P, n // P, P).transpose(2, 1, 0, 3)
        if k // P % UB:
            pad = np.zeros((n // P, P, -(k // P) % UB, P), w.dtype)
            t = np.concatenate([t, pad], axis=2)
        return t.reshape(n // P, P, -1, UB, P).transpose(0, 2, 1, 3, 4)

    win = tiles(w_in)
    q, k, v, g, ca, cb, ga, gb = (win[a // P:b // P] for a, b in zip(
        (0, 1024, 2048, 4096, 6144, 7168, 8192, 9216), (1024, 2048, 4096, 6144, 7168, 8192, 9216, 10240)))
    out = []
    for n in range(KT):
        out += [cb[n], ca[n]]
    for h in range(HEADS):
        out += [*q[2 * h:2 * h + 2], *k[2 * h:2 * h + 2], *v[4 * h:4 * h + 4], *g[4 * h:4 * h + 4]]
    out += list(gb)
    ret = tiles(w_ret_out)
    for n in range(KT):
        out += [ga[n], ret[n]]
    out += [*tiles(w_conv_out), *tiles(w_o)]
    gate, upw = tiles(w_gate), tiles(w_up)
    for n in range(FT):
        out += [gate[n], upw[n]]
    out += list(tiles(w_down))
    return np.concatenate(out)


def kernel(x_prompt, x_sample, state_ret, state_conv, g_mix_pre, g_mix_post, g_ffn_pre, g_ffn_post, w_in, b_gate,
           ret_gn_gain, w_ret_out, conv_w, conv_b, conv_ln_g, conv_ln_b, w_conv_out, w_o, w_ffn_gate, w_ffn_up, w_ffn_down):
    import concourse.bacc as bacc
    from concourse.bass_utils import run_bass_kernel_spmd

    a = {k: np.asarray(v) for k, v in locals().items() if k not in ("bacc", "run_bass_kernel_spmd")}
    feat = lambda v: v.reshape(DEPTH, -1, P).transpose(2, 0, 1)
    x = np.concatenate([a["x_prompt"][0], a["x_sample"].reshape(DB * DS, D)])
    params = np.concatenate(
        [feat(a[k]) for k in ("g_mix_pre", "g_mix_post", "g_ffn_pre", "g_ffn_post", "b_gate", "ret_gn_gain", "conv_b", "conv_ln_g", "conv_ln_b")]
        + [a["conv_w"].reshape(DEPTH, TAPS, KT, P).transpose(3, 0, 2, 1).reshape(P, DEPTH, -1)], axis=2)
    c_in = np.zeros((DEPTH, P, KT, DB, DS + PAD), np.float32)
    c_in[..., 0:PAD] = a["state_conv"].reshape(DEPTH, DB, PAD, KT, P).transpose(0, 4, 3, 1, 2)
    arrays = {
        "w": np.concatenate([units_of(*(a[k][l] for k in ("w_in", "w_ret_out", "w_conv_out", "w_o", "w_ffn_gate", "w_ffn_up", "w_ffn_down")))
                             for l in range(DEPTH)] + [np.zeros((RING, P, UB, P), np.float32)]),
        "xin": x.T.reshape(KT, P, T).transpose(1, 0, 2),
        "consts": constants(),
        "params": np.concatenate([params.transpose(1, 0, 2), np.zeros((1, P, NPAR), np.float32)]),
        "r_in": a["state_ret"].transpose(0, 2, 1, 3, 4).reshape(DEPTH * HEADS * DB, 2, P, DV).transpose(0, 2, 1, 3),
        "c_in": c_in,
    }
    arrays = {k: np.ascontiguousarray(v) for k, v in arrays.items()}
    outs = {
        "x_out": (P, KT, T), "rp_out": (DEPTH * HEADS, P, 2, DV), "rs_out": (DEPTH * HEADS * DB, P, 2, DV),
        "cp_out": (DEPTH, P, KT, SEQ + PAD), "cs_out": (DEPTH, P, KT, DB, DS + PAD),
    }
    nc = bacc.Bacc("TRN2", target_bir_lowering=False, num_devices=1, dynamic_dma_scratch_size=4096)
    args = [nc.dram_tensor(k, v.shape, F32, kind="ExternalInput").ap() for k, v in arrays.items()]
    args += [nc.dram_tensor(k, s, F32, kind="ExternalOutput").ap() for k, s in outs.items()]
    program(nc, *args)
    r = run_bass_kernel_spmd(nc, [arrays], core_ids=[0]).results[0]
    y = r["x_out"].transpose(1, 0, 2).reshape(D, T).T
    rp = r["rp_out"].reshape(DEPTH, 1, HEADS, P, 2, DV).transpose(0, 1, 2, 4, 3, 5).reshape(DEPTH, 1, HEADS, DK, DV)
    rs = r["rs_out"].reshape(DEPTH, HEADS, DB, P, 2, DV).transpose(0, 2, 1, 4, 3, 5).reshape(DEPTH, DB, HEADS, DK, DV)
    cp = r["cp_out"][..., SEQ:].transpose(0, 3, 2, 1).reshape(DEPTH, 1, PAD, D)
    cs = r["cs_out"][..., DS:].transpose(0, 3, 4, 2, 1).reshape(DEPTH, DB, PAD, D)
    return tuple(np.ascontiguousarray(v) for v in (y[:SEQ].reshape(1, SEQ, D), y[SEQ:].reshape(DB, DS, D), rp, cp, rs, cs))
```
